# Optimizing a Trainium2 kernel written in Bass

```python
import jax, jax.numpy as jnp
from jax import lax
import numpy as np

D_MODEL = 1024
BATCH = 1
SEQ = 1024
DEPTH = 1
DEC_BATCH = 8
DEC_SEQ = 16
PAST_LEN = 128

CHUNK = 64
HEAD_DIM = 64
SB_HEADS = 8
SB_BLOCK = 128
SW_HEADS = 8
SW_KV_HEADS = 2
SW_GROUP = SW_HEADS // SW_KV_HEADS
SW_WINDOW = 128
SW_BACK_CHUNKS = SW_WINDOW // CHUNK
MEM_TOKENS = 256
MEM_HEADS = 4
MEM_HEAD_DIM = 128
N_BRANCH = 3
SB_W = SB_HEADS * HEAD_DIM
SW_QW = SW_HEADS * HEAD_DIM
SW_KVW = SW_KV_HEADS * HEAD_DIM
MEM_W = MEM_HEADS * MEM_HEAD_DIM
PROJ_SIZES = (SB_W, SB_W, SB_W, SW_QW, SW_KVW, SW_KVW, MEM_W, N_BRANCH * D_MODEL)
IN_COLS = sum(PROJ_SIZES)
PEER_HEADS = 8
PEER_NKEYS = 128
PEER_EXPERTS = PEER_NKEYS * PEER_NKEYS
PEER_DHALF = 128
PEER_TOPK = 16
PEER_BLOCK = 128
NORM_EPS = 1e-6

kernel_name = 'hybrid_streaming_encoder_step'

def rmsnorm(x, g):
    xf = x.astype(jnp.float32)
    y = xf * lax.rsqrt(jnp.mean(xf * xf, axis=-1, keepdims=True) + NORM_EPS)
    return (y * g.astype(jnp.float32)).astype(x.dtype)

def alibi_slopes(n):
    return jnp.asarray(2.0 ** (-8.0 * np.arange(1, n + 1) / n), dtype=jnp.float32)

def split_projection(h, w_in, b_gate):
    lead = h.shape[:-1]
    cuts = [int(c) for c in np.cumsum(PROJ_SIZES)[:-1]]
    q_sb, k_sb, v_sb, q_sw, k_sw, v_sw, q_mem, g = jnp.split(h @ w_in, cuts, axis=-1)
    gates = jax.nn.sigmoid((g + b_gate).astype(jnp.float32)).astype(h.dtype)
    return (q_sb.reshape(lead + (SB_HEADS, HEAD_DIM)),
            k_sb.reshape(lead + (SB_HEADS, HEAD_DIM)),
            v_sb.reshape(lead + (SB_HEADS, HEAD_DIM)),
            q_sw.reshape(lead + (SW_KV_HEADS, SW_GROUP, HEAD_DIM)),
            k_sw.reshape(lead + (SW_KV_HEADS, HEAD_DIM)),
            v_sw.reshape(lead + (SW_KV_HEADS, HEAD_DIM)),
            q_mem.reshape(lead + (MEM_HEADS, MEM_HEAD_DIM)),
            gates.reshape(lead + (N_BRANCH, D_MODEL)))

def sb_attend(q, k, v, q_pos, k_pos):
    z = jnp.einsum('bqhd,bkhd->bhqk', q, k).astype(jnp.float32) * (HEAD_DIM ** -0.5)
    mask = k_pos[None, :] < q_pos[:, None]
    log_keep = jnp.where(mask, -jax.nn.softplus(z), 0.0)
    log_between = lax.cumsum(log_keep, axis=3, reverse=True) - log_keep
    weight = jnp.where(mask, jnp.exp(jax.nn.log_sigmoid(z) + log_between), 0.0)
    return jnp.einsum('bhqk,bkhd->bqhd', weight.astype(v.dtype), v)

def sw_attend(q, k, v, q_pos, k_pos, sinks):
    logits = jnp.einsum('bcqhgd,bcshd->bhgcqs', q, k).astype(jnp.float32) * (HEAD_DIM ** -0.5)
    dist = jnp.abs(q_pos[:, :, None] - k_pos[:, None, :]).astype(jnp.float32)
    slopes = alibi_slopes(SW_HEADS).reshape(SW_KV_HEADS, SW_GROUP)
    logits = logits - slopes[:, :, None, None, None] * dist
    dchunk = q_pos[:, :, None] // CHUNK - k_pos[:, None, :] // CHUNK
    mask = (k_pos[:, None, :] >= 0) & (dchunk >= 0) & (dchunk <= SW_BACK_CHUNKS)
    logits = jnp.where(mask, logits, -jnp.inf)
    sink = jnp.broadcast_to(sinks.astype(jnp.float32).reshape(SW_KV_HEADS, SW_GROUP, 1, 1, 1),
                            logits.shape[:-1] + (1,))
    p = jax.nn.softmax(jnp.concatenate([logits, sink], axis=-1), axis=-1)[..., :-1]
    return jnp.einsum('bhgcqs,bcshd->bcqhgd', p.astype(v.dtype), v)

def mem_attend(q, k, v):
    s = jnp.einsum('bqhd,bmhd->bhqm', q, k).astype(jnp.float32) * (MEM_HEAD_DIM ** -0.5)
    p = jax.nn.softmax(s, axis=-1)
    return jnp.einsum('bhqm,bmhd->bqhd', p.astype(v.dtype), v)

def memory_kv(mem, norm_mem, w_mem_kv, k_norm_mem):
    lead = mem.shape[:-1]
    k, v = jnp.split(rmsnorm(mem, norm_mem) @ w_mem_kv, 2, axis=-1)
    k = rmsnorm(k.reshape(lead + (MEM_HEADS, MEM_HEAD_DIM)), k_norm_mem)
    return k, v.reshape(lead + (MEM_HEADS, MEM_HEAD_DIM))

def band(a, axis, n_blocks):
    return jnp.concatenate([lax.slice_in_dim(a, j, j + n_blocks, axis=axis)
                            for j in range(SW_BACK_CHUNKS + 1)], axis=axis + 1)

def merge(o_sb, o_sw, o_mem, gates, w_o_sb, w_o_sw, w_o_mem, w_out):
    mixed = (gates[..., 0, :] * (o_sb @ w_o_sb) + gates[..., 1, :] * (o_sw @ w_o_sw)
             + gates[..., 2, :] * (o_mem @ w_o_mem))
    return mixed @ w_out

def peer_block(xb, w_q, pk_keys, u_tab, v_tab):
    t = xb.shape[0]
    q = (xb @ w_q).reshape(t, PEER_HEADS, 2, PEER_DHALF)
    s = jnp.einsum('thpd,hpkd->thpk', q, pk_keys).astype(jnp.float32)
    v1, i1 = lax.top_k(s[:, :, 0], PEER_TOPK)
    v2, i2 = lax.top_k(s[:, :, 1], PEER_TOPK)
    cand = (v1[..., :, None] + v2[..., None, :]).reshape(t, PEER_HEADS, PEER_TOPK * PEER_TOPK)
    best, flat = lax.top_k(cand, PEER_TOPK)
    e1 = jnp.take_along_axis(i1, flat // PEER_TOPK, axis=-1)
    e2 = jnp.take_along_axis(i2, flat % PEER_TOPK, axis=-1)
    idx = e1 * PEER_NKEYS + e2
    g = jax.nn.softmax(best, axis=-1)
    a = jax.nn.gelu(jnp.einsum('thkd,td->thk', u_tab[idx], xb))
    return jnp.einsum('thk,thkd->td', (g * a).astype(xb.dtype), v_tab[idx])

def peer_ffn(x, w_q, pk_keys, u_tab, v_tab):
    lead = x.shape[:-1]
    xt = x.reshape(-1, D_MODEL)
    t = xt.shape[0]
    nb = -(-t // PEER_BLOCK)
    xt = jnp.pad(xt, ((0, nb * PEER_BLOCK - t), (0, 0))).reshape(nb, PEER_BLOCK, D_MODEL)
    out = lax.map(lambda xb: peer_block(xb, w_q, pk_keys, u_tab, v_tab), xt)
    return out.reshape(nb * PEER_BLOCK, D_MODEL)[:t].reshape(lead + (D_MODEL,))

def layer_prompt(x, mem, p):
    (norm_mix, w_in, b_gate, q_norm_sw, k_norm_sw, sinks, norm_mem, w_mem_kv, q_norm_mem,
     k_norm_mem, w_o_sb, w_o_sw, w_o_mem, w_out, norm_ffn, w_peer_q, peer_keys, peer_u, peer_v) = p
    b, s, _ = x.shape
    h = rmsnorm(x, norm_mix)
    q_sb, k_sb, v_sb, q_sw, k_sw, v_sw, q_mem, gates = split_projection(h, w_in, b_gate)
    pos = jnp.arange(s, dtype=jnp.int32)
    nb = s // SB_BLOCK
    qb = q_sb.reshape(b, nb, SB_BLOCK, SB_HEADS, HEAD_DIM).swapaxes(0, 1)
    ob = lax.map(lambda a: sb_attend(a[0], k_sb, v_sb, a[1], pos), (qb, pos.reshape(nb, SB_BLOCK)))
    o_sb = ob.swapaxes(0, 1).reshape(b, s, SB_W)
    q_sw = rmsnorm(q_sw, q_norm_sw)
    k_sw = rmsnorm(k_sw, k_norm_sw)
    nc = s // CHUNK
    back = SW_BACK_CHUNKS * CHUNK
    kp = jnp.pad(k_sw, ((0, 0), (back, 0), (0, 0), (0, 0))).reshape(b, nc + SW_BACK_CHUNKS, CHUNK, SW_KV_HEADS, HEAD_DIM)
    vp = jnp.pad(v_sw, ((0, 0), (back, 0), (0, 0), (0, 0))).reshape(b, nc + SW_BACK_CHUNKS, CHUNK, SW_KV_HEADS, HEAD_DIM)
    kpos = jnp.arange(-back, s, dtype=jnp.int32).reshape(nc + SW_BACK_CHUNKS, CHUNK)
    o_sw = sw_attend(q_sw.reshape(b, nc, CHUNK, SW_KV_HEADS, SW_GROUP, HEAD_DIM),
                     band(kp, 1, nc), band(vp, 1, nc), pos.reshape(nc, CHUNK), band(kpos, 0, nc),
                     sinks).reshape(b, s, SW_QW)
    mk, mv = memory_kv(mem, norm_mem, w_mem_kv, k_norm_mem)
    o_mem = mem_attend(rmsnorm(q_mem, q_norm_mem), mk, mv).reshape(b, s, MEM_W)
    x = x + merge(o_sb, o_sw, o_mem, gates, w_o_sb, w_o_sw, w_o_mem, w_out)
    x = x + peer_ffn(rmsnorm(x, norm_ffn), w_peer_q, peer_keys, peer_u, peer_v)
    return x, k_sb, v_sb, k_sw[:, s - back:], v_sw[:, s - back:], mk, mv

def layer_sample(x, c_sb_k, c_sb_v, c_sw_k, c_sw_v, c_mem_k, c_mem_v, p):
    (norm_mix, w_in, b_gate, q_norm_sw, k_norm_sw, sinks, norm_mem, w_mem_kv, q_norm_mem,
     k_norm_mem, w_o_sb, w_o_sw, w_o_mem, w_out, norm_ffn, w_peer_q, peer_keys, peer_u, peer_v) = p
    b, n, _ = x.shape
    past = c_sb_k.shape[1]
    buf = c_sw_k.shape[1]
    h = rmsnorm(x, norm_mix)
    q_sb, k_sb, v_sb, q_sw, k_sw, v_sw, q_mem, gates = split_projection(h, w_in, b_gate)
    qpos = past + jnp.arange(n, dtype=jnp.int32)
    k_all = jnp.concatenate([c_sb_k, k_sb], axis=1)
    v_all = jnp.concatenate([c_sb_v, v_sb], axis=1)
    o_sb = sb_attend(q_sb, k_all, v_all, qpos, jnp.arange(past + n, dtype=jnp.int32)).reshape(b, n, SB_W)
    q_sw = rmsnorm(q_sw, q_norm_sw)
    k_sw = rmsnorm(k_sw, k_norm_sw)
    kw = jnp.concatenate([c_sw_k, k_sw], axis=1)
    vw = jnp.concatenate([c_sw_v, v_sw], axis=1)
    kpos = jnp.arange(past - buf, past + n, dtype=jnp.int32)
    o_sw = sw_attend(q_sw[:, None], kw[:, None], vw[:, None], qpos[None], kpos[None], sinks).reshape(b, n, SW_QW)
    o_mem = mem_attend(rmsnorm(q_mem, q_norm_mem), c_mem_k, c_mem_v).reshape(b, n, MEM_W)
    x = x + merge(o_sb, o_sw, o_mem, gates, w_o_sb, w_o_sw, w_o_mem, w_out)
    x = x + peer_ffn(rmsnorm(x, norm_ffn), w_peer_q, peer_keys, peer_u, peer_v)
    return x, k_sb, v_sb, kw[:, n:], vw[:, n:]

def setup_inputs(seed: int = 0) -> dict:
    key = jax.random.key(seed)
    ks = jax.random.split(key, 32)
    f32 = jnp.float32

    def nrm(k, shape, scale):
        return jax.random.normal(k, shape, f32) * scale

    def gain(k, n):
        return 1.0 + 0.01 * jax.random.normal(k, (DEPTH, n), f32)

    buf = min(SW_WINDOW, PAST_LEN)
    return {
        'x_prompt': nrm(ks[0], (BATCH, SEQ, D_MODEL), 1.0),
        'mem_prompt': nrm(ks[1], (BATCH, MEM_TOKENS, D_MODEL), 1.0),
        'x_sample': nrm(ks[2], (DEC_BATCH, DEC_SEQ, D_MODEL), 1.0),
        'cache_sb_k': nrm(ks[3], (DEPTH, DEC_BATCH, PAST_LEN, SB_HEADS, HEAD_DIM), 1.0),
        'cache_sb_v': nrm(ks[4], (DEPTH, DEC_BATCH, PAST_LEN, SB_HEADS, HEAD_DIM), 1.0),
        'cache_swa_k': nrm(ks[5], (DEPTH, DEC_BATCH, buf, SW_KV_HEADS, HEAD_DIM), 1.0),
        'cache_swa_v': nrm(ks[6], (DEPTH, DEC_BATCH, buf, SW_KV_HEADS, HEAD_DIM), 1.0),
        'cache_mem_k': nrm(ks[7], (DEPTH, DEC_BATCH, MEM_TOKENS, MEM_HEADS, MEM_HEAD_DIM), 1.0),
        'cache_mem_v': nrm(ks[8], (DEPTH, DEC_BATCH, MEM_TOKENS, MEM_HEADS, MEM_HEAD_DIM), 1.0),
        'norm_mix': gain(ks[9], D_MODEL),
        'w_in': nrm(ks[10], (DEPTH, D_MODEL, IN_COLS), D_MODEL ** -0.5),
        'b_gate': nrm(ks[11], (DEPTH, N_BRANCH * D_MODEL), 0.02),
        'q_norm_sw': gain(ks[12], HEAD_DIM),
        'k_norm_sw': gain(ks[13], HEAD_DIM),
        'sinks': nrm(ks[14], (DEPTH, SW_HEADS), 0.5),
        'norm_mem': gain(ks[15], D_MODEL),
        'w_mem_kv': nrm(ks[16], (DEPTH, D_MODEL, 2 * MEM_W), D_MODEL ** -0.5),
        'q_norm_mem': gain(ks[17], MEM_HEAD_DIM),
        'k_norm_mem': gain(ks[18], MEM_HEAD_DIM),
        'w_o_sb': nrm(ks[19], (DEPTH, SB_W, D_MODEL), SB_W ** -0.5),
        'w_o_sw': nrm(ks[20], (DEPTH, SW_QW, D_MODEL), SW_QW ** -0.5),
        'w_o_mem': nrm(ks[21], (DEPTH, MEM_W, D_MODEL), MEM_W ** -0.5),
        'w_out': nrm(ks[22], (DEPTH, D_MODEL, D_MODEL), D_MODEL ** -0.5),
        'norm_ffn': gain(ks[23], D_MODEL),
        'w_peer_q': nrm(ks[24], (DEPTH, D_MODEL, PEER_HEADS * 2 * PEER_DHALF), D_MODEL ** -0.5),
        'peer_keys': nrm(ks[25], (DEPTH, PEER_HEADS, 2, PEER_NKEYS, PEER_DHALF), PEER_DHALF ** -0.5),
        'peer_u': nrm(ks[26], (DEPTH, PEER_EXPERTS, D_MODEL), D_MODEL ** -0.5),
        'peer_v': nrm(ks[27], (DEPTH, PEER_EXPERTS, D_MODEL), PEER_HEADS ** -0.5),
    }

def reference(x_prompt, mem_prompt, x_sample, cache_sb_k, cache_sb_v, cache_swa_k, cache_swa_v,
              cache_mem_k, cache_mem_v, norm_mix, w_in, b_gate, q_norm_sw, k_norm_sw, sinks,
              norm_mem, w_mem_kv, q_norm_mem, k_norm_mem, w_o_sb, w_o_sw, w_o_mem, w_out,
              norm_ffn, w_peer_q, peer_keys, peer_u, peer_v):
    y_prompt, y_sample = x_prompt, x_sample
    p_sbk, p_sbv, p_swk, p_swv, p_mk, p_mv = [], [], [], [], [], []
    s_sbk, s_sbv, s_swk, s_swv = [], [], [], []
    for l in range(DEPTH):
        p = (norm_mix[l], w_in[l], b_gate[l], q_norm_sw[l], k_norm_sw[l], sinks[l], norm_mem[l],
             w_mem_kv[l], q_norm_mem[l], k_norm_mem[l], w_o_sb[l], w_o_sw[l], w_o_mem[l], w_out[l],
             norm_ffn[l], w_peer_q[l], peer_keys[l], peer_u[l], peer_v[l])
        y_prompt, a, b_, c, d, e, f = layer_prompt(y_prompt, mem_prompt, p)
        p_sbk.append(a); p_sbv.append(b_); p_swk.append(c); p_swv.append(d); p_mk.append(e); p_mv.append(f)
        y_sample, a, b_, c, d = layer_sample(y_sample, cache_sb_k[l], cache_sb_v[l], cache_swa_k[l],
                                             cache_swa_v[l], cache_mem_k[l], cache_mem_v[l], p)
        s_sbk.append(a); s_sbv.append(b_); s_swk.append(c); s_swv.append(d)
    return (y_prompt, y_sample,
            jnp.stack(p_sbk), jnp.stack(p_sbv), jnp.stack(p_swk), jnp.stack(p_swv),
            jnp.stack(p_mk), jnp.stack(p_mv),
            jnp.stack(s_sbk), jnp.stack(s_sbv), jnp.stack(s_swk), jnp.stack(s_swv))


_drawn_inputs = setup_inputs


def setup_inputs(seed=0):
    import zlib

    import numpy as np

    out = dict(_drawn_inputs(seed))
    spreads = {}
    factors = {'norm_mix': 4.4,
     'b_gate': 5.466,
     'q_norm_sw': 8.0,
     'k_norm_sw': 5.645,
     'sinks': 3.933,
     'norm_mem': 5.654,
     'q_norm_mem': 8.0,
     'k_norm_mem': 6.025,
     'norm_ffn': 18.323}
    for name, (base, spread) in spreads.items():
        noise = np.random.default_rng([zlib.crc32(name.encode()), seed]).standard_normal(out[name].shape)
        drawn = base * np.exp(spread * noise) if base else spread * noise
        out[name] = __import__('jax').numpy.asarray(drawn.astype(out[name].dtype))
    for name, factor in factors.items():
        out[name] = (out[name] * factor).astype(out[name].dtype)
    return out
```

```python
from contextlib import ExitStack

import numpy as np

import concourse.bass as bass
from concourse import mybir

ALU = mybir.AluOpType
ACT = mybir.ActivationFunctionType
F32 = mybir.dt.float32
U32 = mybir.dt.uint32
AX = mybir.AxisListType.X

P = 128
DM = 1024
KC = DM // P
PT = 8
ST = PT
NT = PT + 1
TOK = NT * P
DB, DS = 8, 16
HD = 64
MH, MD, MT = 4, 128, 256
SBH, SWH, KVH = 8, 8, 2
GRP = SWH // KVH
SB_W = SBH * HD
GATE0 = 2816
EPS = 1e-6
NEG = -1e30
PH, NK, TOPK = 8, 128, 16
HB = 512
SLOTS = PH * TOPK
RING = 8
BATCH = 4


def host_constants():
    i = np.arange(P)
    k, q = i[:, None], i[None, :]
    ident = np.eye(P)
    tri = -(k >= q).astype(float)
    negones = -np.ones((P, P))
    mask_p = (k < q).astype(float)
    mask_s = ((k // DS == q // DS) & (k < q)).astype(float)
    slopes = 2.0 ** (-8.0 * np.arange(1, SWH + 1) / SWH)
    qn, kn = i[:, None], np.arange(2 * P)[None, :]
    dist = np.abs(qn - kn + P)
    dchunk = (qn + P) // HD - kn // HD
    ok_p = (dchunk >= 0) & (dchunk <= 2)
    dist_s = np.where(kn < P, np.abs(P + qn % DS - kn), np.abs(qn - (kn - P)))
    ok_s = (kn < P) | ((kn - P) // DS == qn // DS)
    def bias(d, ok):
        return np.where(ok[:, None], -slopes[None, :, None] * d[:, None], NEG).reshape(P, -1)
    iota = np.tile(np.arange(TOPK), (P, 1))
    small = np.concatenate([ident, tri, negones, mask_p, mask_s, iota], axis=1).astype(np.float32)
    wide = np.concatenate([bias(dist, ok_p), bias(dist_s, ok_s)], axis=1).astype(np.float32)
    return small, wide


CW = 5 * P + TOPK
BW = SWH * 2 * P


def project(nc, A, S, small_dram):
    ident = S["const"][:, 0:P]
    hT, mhT, ps = S["hT"], S["mhT"], S["ps"]
    with ExitStack() as ctx:
        sb = lambda n, s, dt=F32: ctx.enter_context(nc.sbuf_tensor(n, s, dt))
        sem = lambda n: ctx.enter_context(nc.semaphore(n))
        stage = sb("stage", [P, 4, HB])
        w = sb("w_qkv", [P, 2, KC, HB])
        gmix = sb("gmix", [P, 2, KC])
        gq = sb("gq_heads", [P, 2 * HD + 2 * MD])
        ss = sb("ss", [P, 3])
        nrm = sb("nrm", [P, 3, 8])
        xt = [stage[:, 0:2, :].rearrange("p a n -> p (a n)"), stage[:, 2:4, :].rearrange("p a n -> p (a n)")]
        sqt = stage[:, 3, :]

        const_in = sem("const_in")
        gains_in = sem("gains_in")
        x_in = [sem(f"x_in{i}") for i in range(2)]
        w_in = [sem(f"w_in{i}") for i in range(2)]
        x_sq = sem("x_sq")
        x_ms = sem("x_ms")
        x_rt = sem("x_rt")
        x_rs = sem("x_rs")
        x_nat = sem("x_nat")
        x_T = sem("x_T")
        h_done = sem("h_done")
        proj = sem("proj")
        copied = sem("copied")
        squared = sem("squared")
        summed = sem("summed")
        mean = sem("mean")
        rooted = sem("rooted")
        inverted = sem("inverted")
        scaled = sem("scaled")
        gained = sem("gained")
        turned = sem("turned")
        kept = sem("kept")
        pad_zero = sem("pad_zero")
        nat_out = [sem(f"nat_out{i}") for i in range(3)]
        v_out = sem("v_out")
        cache_out = sem("cache_out")

        TILES = [A["x_prompt"][0, t * P:(t + 1) * P, :] for t in range(PT)]
        TILES += [A["x_sample"].rearrange("b s d -> (b s) d")]
        TILES += [A["mem_prompt"][0, t * P:(t + 1) * P, :] for t in range(2)]
        NX = len(TILES)

        w_v = A["w_in"][0].rearrange("(c p) n -> p c n", p=P)
        wm_v = A["w_mem_kv"][0].rearrange("(c p) n -> p c n", p=P)
        BLOCKS = [("ksb", w_v[:, :, 512:1024], 512, range(NT)), ("vsb", w_v[:, :, 1024:1536], 512, range(NT)),
                  ("kvsw", w_v[:, :, 2048:2304], 256, range(NT)), ("qsw", w_v[:, :, 1536:2048], 512, range(NT)),
                  ("qm", w_v[:, :, 2304:2816], 512, range(NT)), ("mk", wm_v[:, :, 0:512], 512, range(2)),
                  ("mv", wm_v[:, :, 512:1024], 512, range(2)), ("qsb", w_v[:, :, 0:512], 512, range(12))]
        units = [(c, kind, t) for c, (kind, _, _, tiles) in enumerate(BLOCKS) for t in tiles]
        n_copy, n_norm, n_turn = [], [], []
        a = b = d = 0
        slots, s = [], 0
        n_out = [0, 0, 0]
        outs_before = []
        for _, kind, t in units:
            a += kind in ("ksb", "vsb", "mv", "qsb", "kvsw")
            b += kind in ("kvsw", "qsw", "qm", "mk")
            turns = kind in ("ksb", "kvsw", "qsw", "qm", "mk")
            d += turns
            n_copy.append(a)
            n_norm.append(b)
            n_turn.append(d)
            slots.append(s % 3 if turns else None)
            outs_before.append(n_out[s % 3] if turns else 0)
            if turns:
                if kind in ("ksb", "mk"):
                    n_out[s % 3] += 1
                if kind == "kvsw" and t == PT - 1:
                    n_out[s % 3] += 1
                if kind == "kvsw" and t == ST:
                    n_out[s % 3] += DB
                s += 1
        FINAL_OUT = list(n_out)
        last_of = {c: max(u for u, x in enumerate(units) if x[0] == c) for c in range(len(BLOCKS))}
        copies = ("ksb", "vsb", "mv", "qsb", "kvsw")
        norms = ("kvsw", "qsw", "qm", "mk")
        heads = {"kvsw": (KVH, HD), "qsw": (SWH, HD), "qm": (MH, MD), "mk": (MH, MD)}
        gain_of = {"qsw": gq[:, 0:HD], "kvsw": gq[:, HD:2 * HD], "qm": gq[:, 2 * HD:2 * HD + MD],
                   "mk": gq[:, 2 * HD + MD:2 * HD + 2 * MD]}
        NPB = 3

        def bank(u):
            return u % NPB

        def turn_bank(n):
            return 3 + n % 2

        block = ctx.enter_context(nc.Block())

        @block.sync
        def _(sp):
            sp.dma_start(S["const"][:, :], small_dram[:, :]).then_inc(const_in, 16)
            with nc.allow_non_contiguous_dma(reason="gains, a few kilobytes"):
                sp.dma_start(gmix[:, 0, :], A["norm_mix"][0].rearrange("(c p) -> p c", p=P)).then_inc(gains_in, 16)
                sp.dma_start(gmix[:, 1, :], A["norm_mem"][0].rearrange("(c p) -> p c", p=P)).then_inc(gains_in, 16)
            o = 0
            for name, n in (("q_norm_sw", HD), ("k_norm_sw", HD), ("q_norm_mem", MD), ("k_norm_mem", MD)):
                sp.dma_start(gq[:, o:o + n], A[name][0:1, :].to_broadcast([P, n])).then_inc(gains_in, 16)
                o += n

            def load_w(c):
                if c >= 2:
                    sp.wait_ge(proj, last_of[c - 2] + 1)
                n = BLOCKS[c][2]
                sp.dma_start(w[:, c % 2, :, 0:n], BLOCKS[c][1]).then_inc(w_in[c % 2], 16)

            for t in range(NX):
                if t >= 2:
                    sp.wait_ge(x_T, t - 1)
                sp.dma_start(xt[t % 2], TILES[t]).then_inc(x_in[t % 2], 16)
                if t in (1, 2):
                    load_w(t - 1)
            for name, c in (("new_swa_k_sample", "cache_swa_k"), ("new_swa_v_sample", "cache_swa_v")):
                sp.dma_start(A[name][0, :, 0:P - DS].rearrange("b s h d -> b (s h d)"),
                             A[c][0, :, DS:P].rearrange("b s h d -> b (s h d)")).then_inc(cache_out, 16)
            nv = 0
            at = 2
            for u, (c, kind, t) in enumerate(units):
                if at < len(BLOCKS) and at == c + 1 and t == 0 and c >= 1:
                    load_w(at)
                    at += 1
                rows = slice(t * P, (t + 1) * P)
                q = slots[u]
                if kind == "ksb":
                    sp.wait_ge(copied, n_copy[u])
                    dst = A["new_sb_k_prompt"][0, 0, rows] if t < ST else A["new_sb_k_sample"][0].rearrange("b s h d -> (b s) h d")
                    sp.dma_start(dst.rearrange("s h d -> s (h d)"), stage[:, q, :]).then_inc(nat_out[q], 16)
                if kind == "vsb":
                    sp.wait_ge(copied, n_copy[u])
                    dst = A["new_sb_v_prompt"][0, 0, rows] if t < ST else A["new_sb_v_sample"][0].rearrange("b s h d -> (b s) h d")
                    sp.dma_start(dst.rearrange("s h d -> s (h d)"), S["vsb"][:, t, :]).then_inc(v_out, 16)
                    nv += 1
                if kind == "mk":
                    sp.wait_ge(gained, n_norm[u])
                    sp.dma_start(A["new_mem_k_prompt"][0, 0, rows].rearrange("s h d -> s (h d)"), stage[:, q, :]).then_inc(nat_out[q], 16)
                if kind == "mv":
                    sp.wait_ge(copied, n_copy[u])
                    sp.dma_start(A["new_mem_v_prompt"][0, 0, rows].rearrange("s h d -> s (h d)"), S["mv"][:, t, :]).then_inc(v_out, 16)
                    nv += 1
                if kind == "kvsw" and t == PT - 1:
                    sp.wait_ge(gained, n_norm[u])
                    sp.dma_start(A["new_swa_k_prompt"][0, 0].rearrange("s h d -> s (h d)"), stage[:, q, 0:P]).then_inc(nat_out[q], 16)
                    sp.wait_ge(copied, n_copy[u])
                    sp.dma_start(A["new_swa_v_prompt"][0, 0].rearrange("s h d -> s (h d)"), S["vsw"][:, t + 1, :]).then_inc(v_out, 16)
                    nv += 1
                if kind == "kvsw" and t == ST:
                    sp.wait_ge(gained, n_norm[u])
                    sp.wait_ge(copied, n_copy[u])
                    for b in range(DB):
                        r = slice(b * DS, (b + 1) * DS)
                        sp.dma_start(A["new_swa_k_sample"][0, b, P - DS:P].rearrange("s h d -> s (h d)"), stage[r, q, 0:P]).then_inc(nat_out[q], 16)
                        sp.dma_start(A["new_swa_v_sample"][0, b, P - DS:P].rearrange("s h d -> s (h d)"), S["vsw"][r, t + 1, :]).then_inc(v_out, 16)
                        nv += 1
            for q in range(3):
                sp.wait_ge(nat_out[q], 16 * FINAL_OUT[q])
            sp.wait_ge(v_out, 16 * nv)
            sp.wait_ge(cache_out, 32)

        @block.gpsimd
        def _(pool):
            nc.gpsimd.memset(S["kswT"][:, 0:P], 0.0).then_inc(pad_zero, 1)
            nc.gpsimd.memset(S["vsw"][:, 0, :], 0.0).then_inc(pad_zero, 1)
            pool.wait_ge(pad_zero, 2)

        @block.tensor
        def _(pe):
            pe.wait_ge(const_in, 16)
            for t in range(NX):
                pe.wait_ge(x_nat, t + 1)
                if t >= 2:
                    pe.wait_ge(h_done, t - 1)
                for c in range(KC):
                    last = nc.tensor.transpose(ps[:, 4 + 2 * (t % 2) + c // 4, (c % 4) * P:(c % 4 + 1) * P],
                                               xt[t % 2][:, c * P:(c + 1) * P], ident)
                last.then_inc(x_T, 1)
            pe.wait_ge(h_done, NX)

            def turn(u):
                c, kind, t = units[u]
                if slots[u] is None:
                    return
                n = n_turn[u] - 1
                if n >= 2:
                    pe.wait_ge(kept, n - 1)
                if kind == "ksb":
                    pe.wait_ge(copied, n_copy[u])
                else:
                    pe.wait_ge(gained, n_norm[u])
                m = 1 if kind == "kvsw" else 4
                for j in range(m):
                    last = nc.tensor.transpose(ps[:, turn_bank(n), j * P:(j + 1) * P], stage[:, slots[u], j * P:(j + 1) * P], ident)
                last.then_inc(turned, 1)

            for u, (c, kind, t) in enumerate(units):
                if t == 0:
                    pe.wait_ge(w_in[c % 2], 16 * (c // 2 + 1))
                if u >= NPB:
                    if units[u - NPB][1] in copies:
                        pe.wait_ge(copied, n_copy[u - NPB])
                    if units[u - NPB][1] in norms:
                        pe.wait_ge(scaled, n_norm[u - NPB])
                for k in range(KC):
                    if kind == "qsb":
                        j, g = t // 3, t % 3
                        last = nc.tensor.matmul(ps[:, bank(u), 0:3 * P], w[:, c % 2, k, j * P:(j + 1) * P],
                                                hT[:, k, g * 3 * P:(g + 1) * 3 * P], start=(k == 0), stop=(k == KC - 1))
                    else:
                        n = BLOCKS[c][2]
                        src = mhT if kind in ("mk", "mv") else hT
                        last = nc.tensor.matmul(ps[:, bank(u), 0:n], src[:, k, t * P:(t + 1) * P], w[:, c % 2, k, 0:n],
                                                start=(k == 0), stop=(k == KC - 1))
                last.then_inc(proj, 1)
                if u >= 2:
                    turn(u - 2)
            turn(len(units) - 2)
            turn(len(units) - 1)

        @block.scalar
        def _(act):
            for t in range(NX):
                act.wait_ge(x_in[t % 2], 16 * (t // 2 + 1))
                if t >= 1:
                    act.wait_ge(x_sq, t)
                nc.scalar.activation(ps[:, 0:2, :].rearrange("p a n -> p (a n)"), xt[t % 2], ACT.Square,
                                     accum_out=ss[:, 0:1]).then_inc(x_sq, 1)
                act.wait_ge(x_ms, t + 1)
                nc.scalar.activation(ss[:, 2:3], ss[:, 1:2], ACT.Sqrt).then_inc(x_rt, 1)
            act.wait_ge(pad_zero, 2)

            def keep(u):
                c, kind, t = units[u]
                if slots[u] is None:
                    return
                act.wait_ge(turned, n_turn[u])
                src = ps[:, turn_bank(n_turn[u] - 1), :].rearrange("p (j n) -> p j n", j=4)
                cols = slice(t * P, (t + 1) * P)
                if kind == "ksb":
                    i = nc.scalar.activation(S["ksbT"][:, :, cols], src, ACT.Copy)
                elif kind == "kvsw":
                    i = nc.scalar.activation(S["kswT"][:, (t + 1) * P:(t + 2) * P], src[:, 0, :], ACT.Copy)
                elif kind == "qsw":
                    i = nc.scalar.activation(S["qswT"][:, :, cols], src, ACT.Copy, scale=HD ** -0.5)
                elif kind == "qm":
                    i = nc.scalar.activation(S["qmT"][:, :, cols], src, ACT.Copy)
                else:
                    i = nc.scalar.activation(S["mkT"][:, :, cols], src, ACT.Copy)
                i.then_inc(kept, 1)

            for u, (c, kind, t) in enumerate(units):
                act.wait_ge(proj, u + 1)
                src = ps[:, bank(u), :]
                if kind in norms:
                    H, D = heads[kind]
                    if n_norm[u] > 1:
                        act.wait_ge(summed, n_norm[u] - 1)
                    nc.scalar.activation(sqt[:, 0:H * D], src[:, 0:H * D], ACT.Square).then_inc(squared, 1)
                if kind in copies:
                    if kind == "ksb":
                        if n_turn[u] > 3:
                            act.wait_ge(turned, n_turn[u] - 3)
                            act.wait_ge(nat_out[slots[u]], 16 * outs_before[u])
                        i = nc.scalar.activation(stage[:, slots[u], :], src, ACT.Copy)
                    elif kind == "vsb":
                        i = nc.scalar.activation(S["vsb"][:, t, :], src, ACT.Copy)
                    elif kind == "mv":
                        i = nc.scalar.activation(S["mv"][:, t, :], src, ACT.Copy)
                    elif kind == "kvsw":
                        i = nc.scalar.activation(S["vsw"][:, t + 1, :], src[:, P:2 * P], ACT.Copy)
                    else:
                        j, g = t // 3, t % 3
                        i = nc.scalar.activation(S["qsbT"][:, j, g * 3 * P:(g + 1) * 3 * P], src[:, 0:3 * P], ACT.Copy, scale=HD ** -0.5)
                    i.then_inc(copied, 1)
                if kind in norms:
                    act.wait_ge(mean, n_norm[u])
                    H, D = heads[kind]
                    nc.scalar.activation(nrm[:, 1, 0:H], nrm[:, 0, 0:H], ACT.Sqrt).then_inc(rooted, 1)
                if u >= 2:
                    keep(u - 2)
            keep(len(units) - 2)
            keep(len(units) - 1)

        @block.vector
        def _(dve):
            dve.wait_ge(gains_in, 16 * 6)
            for t in range(NX + 1):
                if t < NX:
                    dve.wait_ge(x_sq, t + 1)
                    if t >= 1:
                        dve.wait_ge(x_rt, t)
                    nc.vector.tensor_scalar(ss[:, 1:2], ss[:, 0:1], 1.0 / DM, EPS, ALU.mult, ALU.add).then_inc(x_ms, 1)
                    dve.wait_ge(x_rt, t + 1)
                    nc.vector.reciprocal(nrm[:, 2, 0:1], ss[:, 2:3]).then_inc(x_rs, 1)
                    dve.wait_ge(x_rs, t + 1)
                    nc.vector.tensor_scalar(xt[t % 2], xt[t % 2], nrm[:, 2, 0:1], None, ALU.mult).then_inc(x_nat, 1)
                if t >= 1:
                    v = t - 1
                    dve.wait_ge(x_T, v + 1)
                    b = 4 + 2 * (v % 2)
                    src = ps[:, b:b + 2, :].rearrange("p a (c n) -> p (a c) n", n=P)
                    if v < NT:
                        dst, g = hT[:, :, v * P:(v + 1) * P], gmix[:, 0, :]
                    else:
                        dst, g = mhT[:, :, (v - NT) * P:(v - NT + 1) * P], gmix[:, 1, :]
                    nc.vector.tensor_tensor(dst, src, g.unsqueeze(2).to_broadcast([P, KC, P]), ALU.mult).then_inc(h_done, 1)
            for u, (c, kind, t) in enumerate(units):
                if kind not in norms:
                    continue
                H, D = heads[kind]
                n = n_norm[u]
                dve.wait_ge(squared, n)
                if n > 1:
                    dve.wait_ge(inverted, n - 1)
                nc.vector.tensor_reduce(nrm[:, 2, 0:H], sqt[:, 0:H * D].rearrange("p (h d) -> p h d", h=H), AX, ALU.add).then_inc(summed, 1)
                dve.wait_ge(summed, n)
                nc.vector.tensor_scalar(nrm[:, 0, 0:H], nrm[:, 2, 0:H], 1.0 / D, EPS, ALU.mult, ALU.add).then_inc(mean, 1)
                dve.wait_ge(rooted, n)
                nc.vector.reciprocal(nrm[:, 2, 0:H], nrm[:, 1, 0:H]).then_inc(inverted, 1)
                dve.wait_ge(inverted, n)
                dve.wait_ge(proj, u + 1)
                if n_turn[u] > 3:
                    dve.wait_ge(turned, n_turn[u] - 3)
                    if outs_before[u]:
                        dve.wait_ge(nat_out[slots[u]], 16 * outs_before[u])
                nat = stage[:, slots[u], 0:H * D]
                if kind == "qsw":
                    out = nat.rearrange("p (j g d) -> p g j d", g=KVH, j=GRP)
                    src = ps[:, bank(u), 0:H * D].rearrange("p (g j d) -> p g j d", g=KVH, j=GRP)
                    r = nrm[:, 2, 0:H].rearrange("p (g j) -> p g j", g=KVH).unsqueeze(3).to_broadcast([P, KVH, GRP, D])
                else:
                    out = nat.rearrange("p (h d) -> p h d", h=H)
                    src = ps[:, bank(u), 0:H * D].rearrange("p (h d) -> p h d", h=H)
                    r = nrm[:, 2, 0:H].unsqueeze(2).to_broadcast([P, H, D])
                nc.vector.tensor_tensor(out, src, r, ALU.mult).then_inc(scaled, 1)
                dve.wait_ge(scaled, n)
                flat = nat.rearrange("p (h d) -> p h d", h=H)
                nc.vector.tensor_tensor(flat, flat, gain_of[kind].unsqueeze(1).to_broadcast([P, H, D]), ALU.mult).then_inc(gained, 1)


def stick(nc, A, S):
    ident, tri, negones = (S["const"][:, i * P:(i + 1) * P] for i in range(3))
    masks = [S["const"][:, 3 * P:4 * P], S["const"][:, 4 * P:5 * P]]
    qT, kT, v, ps = S["qsbT"], S["ksbT"], S["vsb"], S["ps"]
    steps = [(t, kb, kb == t, kb == 0) for t in range(PT) for kb in range(t, -1, -1)]
    steps += [(ST, ST, True, False), (ST, None, False, True)]
    N = len(steps)
    W8 = SBH * P
    with ExitStack() as ctx:
        sb = lambda n, s: ctx.enter_context(nc.sbuf_tensor(n, s, F32))
        sem = lambda n: ctx.enter_context(nc.semaphore(n))
        za = sb("za", [P, 2, W8])
        zc = sb("zc", [P, 2, W8])
        sp_ = sb("sp", [P, 2, W8])
        later = sb("later", [P, 2, W8])
        kc = sb("kc", [P, 2, SB_W])
        kcT = sb("kcT", [P, DB, 4, P])
        kc_in = [sem(f"kc_in{i}") for i in range(2)]
        vc_in = sem("vc_in")
        kc_T = sem("kc_T")
        kc_kept = sem("kc_kept")
        logits = sem("logits")
        absd = sem("absd")
        exped = sem("exped")
        logd = sem("logd")
        zcopied = sem("zcopied")
        sp_raw = sem("sp_raw")
        sp_ready = sem("sp_ready")
        later_ready = sem("later_ready")
        sums = sem("sums")
        expo = sem("expo")
        added = sem("added")
        weight = sem("weight")
        masked = sem("masked")
        pv = sem("pv")
        o_kept = sem("o_kept")
        diag = [sum(s[2] for s in steps[:n + 1]) for n in range(N)]
        ends = [sum(s[3] for s in steps[:n + 1]) for n in range(N)]

        def vcache(b):
            return kT[:, b // 2, (b % 2) * SB_W:(b % 2 + 1) * SB_W]

        block = ctx.enter_context(nc.Block())

        @block.sync
        def _(sp):
            for b in range(DB):
                if b >= 2:
                    sp.wait_ge(kc_T, b - 1)
                sp.dma_start(kc[:, b % 2, :], A["cache_sb_k"][0, b].rearrange("s h d -> s (h d)")).then_inc(kc_in[b % 2], 16)
            sp.wait_ge(logits, N - 2)
            for b in range(DB):
                sp.dma_start(vcache(b), A["cache_sb_v"][0, b].rearrange("s h d -> s (h d)")).then_inc(vc_in, 16)

        @block.tensor
        def _(pe):
            for b in range(DB):
                pe.wait_ge(kc_in[b % 2], 16 * (b // 2 + 1))
                if b >= 4:
                    pe.wait_ge(kc_kept, b - 3)
                for j in range(4):
                    last = nc.tensor.transpose(ps[:, b % 4, j * P:(j + 1) * P], kc[:, b % 2, j * P:(j + 1) * P], ident)
                last.then_inc(kc_T, 1)
            pe.wait_ge(kc_kept, DB)

            def score(n):
                t, kb, _, _ = steps[n]
                if n >= 2:
                    pe.wait_ge(zcopied, n - 1)
                    pe.wait_ge(sp_raw, n - 1)
                for h in range(SBH):
                    r = slice((h % 2) * HD, (h % 2 + 1) * HD)
                    o = ps[:, 2 * (n % 2) + h % 2, (h // 2) * P:(h // 2 + 1) * P]
                    if kb is not None:
                        last = nc.tensor.matmul(o, kT[r, h // 2, kb * P:(kb + 1) * P], qT[r, h // 2, t * P:(t + 1) * P],
                                                start=True, stop=True)
                        continue
                    for b in range(DB):
                        c = slice(b * DS, (b + 1) * DS)
                        last = nc.tensor.matmul(o[:, c], kcT[r, b, h // 2, :], qT[r, h // 2, t * P + b * DS:t * P + (b + 1) * DS],
                                                start=True, stop=True)
                last.then_inc(logits, 1)

            def suffix(n):
                first = steps[n][2]
                pe.wait_ge(sp_ready, n + 1)
                if n >= 1:
                    pe.wait_ge(expo, n)
                if not first:
                    pe.wait_ge(later_ready, n)
                for i in range(2):
                    last = nc.tensor.matmul(ps[:, 4 + i, :], tri, sp_[:, n % 2, i * HB:(i + 1) * HB], start=True, stop=first)
                    if not first:
                        last = nc.tensor.matmul(ps[:, 4 + i, :], negones, later[:, (n - 1) % 2, i * HB:(i + 1) * HB],
                                                start=False, stop=True)
                last.then_inc(sums, 1)

            def values(n):
                t, kb, first, end = steps[n]
                if first:
                    pe.wait_ge(masked, diag[n])
                    if t >= 2:
                        pe.wait_ge(o_kept, t - 1)
                else:
                    pe.wait_ge(weight, n + 1)
                if kb is None:
                    pe.wait_ge(vc_in, 16 * DB)
                w = zc[:, n % 2, :]
                for h in range(SBH):
                    at = ((h % 2) * (SBH // 2) + h // 2) * P
                    o = ps[(h % 2) * HD:(h % 2 + 1) * HD, 6 + t % 2, (h // 2) * P:(h // 2 + 1) * P]
                    if kb is not None:
                        last = nc.tensor.matmul(o, v[:, kb, h * HD:(h + 1) * HD], w[:, at:at + P],
                                                start=first and h < 2, stop=end, skip_group_check=True)
                        continue
                    for b in range(DB):
                        last = nc.tensor.matmul(o[:, b * DS:(b + 1) * DS], vcache(b)[:, h * HD:(h + 1) * HD],
                                                w[:, at + b * DS:at + (b + 1) * DS], start=False, stop=True,
                                                skip_group_check=True)
                last.then_inc(pv, 1)

            score(0)
            for n in range(N):
                if n + 1 < N:
                    score(n + 1)
                suffix(n)
                if n >= 1:
                    values(n - 1)
            values(N - 1)

        @block.scalar
        def _(act):
            nc.scalar.preload_act_table_set("natural_log_exp_and_others")
            for b in range(DB):
                act.wait_ge(kc_T, b + 1)
                nc.scalar.activation(kcT[:, b], ps[:, b % 4, :].rearrange("p (j n) -> p j n", j=4), ACT.Copy).then_inc(kc_kept, 1)

            def weigh(n):
                act.wait_ge(expo, n + 1)
                nc.scalar.activation(zc[:, n % 2, :], zc[:, n % 2, :], ACT.Exp).then_inc(weight, 1)

            for n in range(N):
                z = ps[:, 2 * (n % 2):2 * (n % 2) + 2, :].rearrange("p a n -> p (a n)")
                act.wait_ge(logits, n + 1)
                if n >= 2:
                    act.wait_ge(sp_raw, n - 1)
                    act.wait_ge(pv, n - 1)
                nc.scalar.activation(za[:, n % 2, :], z, ACT.Abs).then_inc(absd, 1)
                nc.scalar.activation(zc[:, n % 2, :], z, ACT.Copy).then_inc(zcopied, 1)
                act.wait_ge(absd, n + 1)
                nc.scalar.activation(za[:, n % 2, :], za[:, n % 2, :], ACT.Exp, scale=-1.0).then_inc(exped, 1)
                act.wait_ge(exped, n + 1)
                nc.scalar.activation(za[:, n % 2, :], za[:, n % 2, :], ACT.Ln, bias=1.0).then_inc(logd, 1)
                if n >= 1:
                    weigh(n - 1)
            weigh(N - 1)

        @block.gpsimd
        def _(pool):
            def later_sum(n):
                pool.wait_ge(sp_ready, n + 1)
                if n >= 2:
                    pool.wait_ge(sums, n)
                if n >= 1:
                    pool.wait_ge(later_ready, n)
                if steps[n][2]:
                    nc.gpsimd.tensor_copy(later[:, n % 2, :], sp_[:, n % 2, :]).then_inc(later_ready, 1)
                else:
                    nc.gpsimd.tensor_tensor(later[:, n % 2, :], later[:, (n - 1) % 2, :], sp_[:, n % 2, :], ALU.add).then_inc(later_ready, 1)

            def mask_weight(n):
                if steps[n][2]:
                    m = masks[steps[n][0] == ST].unsqueeze(1).to_broadcast([P, SBH, P])
                    w = zc[:, n % 2, :].rearrange("p (h q) -> p h q", h=SBH)
                    pool.wait_ge(weight, n + 1)
                    nc.gpsimd.tensor_tensor(w, w, m, ALU.mult).then_inc(masked, 1)

            for n in range(N):
                later_sum(n)
                if n >= 1:
                    mask_weight(n - 1)

        @block.vector
        def _(dve):
            def soft(n):
                t, _, first, _ = steps[n]
                z = ps[:, 2 * (n % 2):2 * (n % 2) + 2, :].rearrange("p a n -> p (a n)")
                s = sp_[:, n % 2, :]
                dve.wait_ge(logd, n + 1)
                if n >= 2:
                    dve.wait_ge(sums, n - 1)
                    dve.wait_ge(later_ready, n - 1)
                i = nc.vector.scalar_tensor_tensor(out=s, in0=z, scalar=0.0, in1=za[:, n % 2, :], op0=ALU.max, op1=ALU.add)
                i.then_inc(sp_raw, 1)
                dve.wait_ge(sp_raw, n + 1)
                if first:
                    m = masks[t == ST].unsqueeze(1).to_broadcast([P, SBH, P])
                    s3 = s.rearrange("p (h q) -> p h q", h=SBH)
                    nc.vector.tensor_tensor(s3, s3, m, ALU.mult).then_inc(sp_ready, 1)
                else:
                    dve.sem_inc(sp_ready, 1)

            def exponent(n):
                dve.wait_ge(sums, n + 1)
                dve.wait_ge(zcopied, n + 1)
                c = zc[:, n % 2, :]
                nc.vector.tensor_tensor(c, c, ps[:, 4:6, :].rearrange("p a n -> p (a n)"), ALU.add).then_inc(added, 1)
                dve.wait_ge(added, n + 1)
                if steps[n][2]:
                    nc.vector.tensor_scalar(c, c, 0.0, None, ALU.min).then_inc(expo, 1)
                else:
                    dve.sem_inc(expo, 1)

            def keep(n):
                t, _, _, end = steps[n]
                if end:
                    dve.wait_ge(pv, n + 1)
                    nc.vector.tensor_copy(qT[:, :, t * P:(t + 1) * P], ps[:, 6 + t % 2, :].rearrange("p (j n) -> p j n", j=4)).then_inc(o_kept, 1)

            for n in range(N):
                soft(n)
                if n >= 1:
                    exponent(n - 1)
                if n >= 2:
                    keep(n - 2)
            exponent(N - 1)
            keep(N - 2)
            keep(N - 1)


def windows(nc, A, S, wide_dram):
    ident, ps = S["const"][:, 0:P], S["ps"]
    qw, kw, vw, qm, mk, mv = S["qswT"], S["kswT"], S["vsw"], S["qmT"], S["mkT"], S["mv"]
    units = [(t, g) for t in range(NT) for g in (0, 1, 2)]
    N = len(units)
    W = 4 * 2 * P
    RL = 3
    with ExitStack() as ctx:
        sb = lambda n, s: ctx.enter_context(nc.sbuf_tensor(n, s, F32))
        sem = lambda n: ctx.enter_context(nc.semaphore(n))
        bias = sb("bias", [P, 2, SWH, 2 * P])
        sink = sb("sink", [P, SWH])
        L = sb("L", [P, RL, 4, 2 * P])
        PTs = sb("PTs", [P, 2, W])
        past_w = sb("past_w", [P, SWH, P])
        past_m = sb("past_m", [P, 2, MH, P])
        kwc = sb("kwc", [P, DB, P])
        kwcT = sb("kwcT", [P, 2, P])
        vwc = sb("vwc", [P, DB, P])
        big = sb("big", [P, DB, 2 * MH * MD])
        mx = sb("mx", [P, RL, 8, 4])
        bias_in = sem("bias_in")
        kw_in = sem("kw_in")
        km_in = [sem(f"km_in{i}") for i in range(2)]
        vm_in = sem("vm_in")
        cT = sem("cT")
        cKept = sem("cKept")
        cMul = sem("cMul")
        cOut = sem("cOut")
        logits = sem("w_logits")
        biased = sem("biased")
        padded = sem("padded")
        maxed = sem("maxed")
        sunk = sem("sunk")
        negd = sem("negd")
        exped = sem("w_exped")
        total = sem("total")
        inv = sem("inv")
        normed = sem("normed")
        turned = sem("w_turned")
        pt_kept = sem("pt_kept")
        pv = sem("w_pv")
        o_kept = sem("w_o_kept")
        n_win = [sum(g < 2 for _, g in units[:u + 1]) for u in range(N)]

        kview = A["cache_mem_k"][0].rearrange("b (k p) h d -> b p k (h d)", p=P)
        vview = A["cache_mem_v"][0].rearrange("b (k p) h d -> b p k (h d)", p=P)
        two = lambda x: x.rearrange("p (k n) -> p k n", k=2)
        block = ctx.enter_context(nc.Block())

        @block.sync
        def _(sp):
            sp.dma_start(bias[:, :, :, :].rearrange("p a h k -> p (a h k)"), wide_dram[:, :]).then_inc(bias_in, 16)
            sp.dma_start(sink[:, :], A["sinks"][0:1, :].to_broadcast([P, SWH])).then_inc(bias_in, 16)
            sp.dma_start(kwc[:, :, :], A["cache_swa_k"][0].rearrange("b s h d -> s b (h d)")).then_inc(kw_in, 16)
            sp.dma_start(vwc[:, :, :], A["cache_swa_v"][0].rearrange("b s h d -> s b (h d)")).then_inc(kw_in, 16)
            for b in range(DB):
                if b >= 2:
                    sp.wait_ge(cT, b - 1)
                sp.dma_start(two(big[:, b % 2, :]), kview[b]).then_inc(km_in[b % 2], 16)
            sp.wait_ge(cMul, DB)
            for b in range(DB):
                sp.dma_start(two(big[:, b, :]), vview[b]).then_inc(vm_in, 16)

        @block.tensor
        def _(pe):
            pe.wait_ge(kw_in, 32)
            for b in range(DB):
                pe.wait_ge(km_in[b % 2], 16 * (b // 2 + 1))
                if b >= 1:
                    pe.wait_ge(cKept, b)
                for j in range(8):
                    nc.tensor.transpose(ps[:, j // 4, (j % 4) * P:(j % 4 + 1) * P], big[:, b % 2, j * P:(j + 1) * P], ident)
                nc.tensor.transpose(ps[:, 2, 0:P], kwc[:, b, :], ident).then_inc(cT, 1)
                pe.wait_ge(cKept, b + 1)
                c = slice(ST * P + b * DS, ST * P + (b + 1) * DS)
                for k in range(2):
                    for h in range(MH):
                        nc.tensor.matmul(ps[:, 4 + k, h * P + b * DS:h * P + (b + 1) * DS],
                                         big[:, 2 + b % 2, (k * MH + h) * P:(k * MH + h + 1) * P], qm[:, h, c], start=True, stop=True)
                for h in range(SWH):
                    g, j = h // GRP, h % GRP
                    r = slice(g * HD, (g + 1) * HD)
                    last = nc.tensor.matmul(ps[:, 6 + g, j * P + b * DS:j * P + (b + 1) * DS], kwcT[r, b % 2, :], qw[r, j, c],
                                            start=True, stop=True)
                last.then_inc(cMul, 1)
            pe.wait_ge(cOut, 2)

            def scores(u):
                t, g = units[u]
                if u >= 2:
                    pe.wait_ge(exped, u - 1)
                    pe.wait_ge(maxed, u - 1)
                o = ps[:, 2 * (u % 2):2 * (u % 2) + 2, :].rearrange("p a (j k) -> p (a j) k", k=2 * P)
                for j in range(4):
                    r = slice((g % 2) * HD, (g % 2 + 1) * HD)
                    if g < 2 and t < ST:
                        last = nc.tensor.matmul(o[:, j, :], qw[r, j, t * P:(t + 1) * P], kw[r, t * P:(t + 2) * P], start=True, stop=True)
                    elif g < 2:
                        nc.tensor.transpose(o[:, j, 0:P], past_w[:, g * GRP + j, :], ident)
                        last = nc.tensor.matmul(o[:, j, P:2 * P], qw[r, j, t * P:(t + 1) * P], kw[r, NT * P:(NT + 1) * P], start=True, stop=True)
                    elif t < ST:
                        last = nc.tensor.matmul(o[:, j, :], qm[:, j, t * P:(t + 1) * P], mk[:, j, :], start=True, stop=True)
                    else:
                        for k in range(2):
                            last = nc.tensor.transpose(o[:, j, k * P:(k + 1) * P], past_m[:, k, j, :], ident)
                last.then_inc(logits, 1)

            def turn(u):
                pe.wait_ge(normed, u + 1)
                if u >= 1:
                    pe.wait_ge(pt_kept, u)
                for i in range(8):
                    last = nc.tensor.transpose(ps[:, 4 + i // 4, (i % 4) * P:(i % 4 + 1) * P], L[:, u % RL, i // 2, (i % 2) * P:(i % 2 + 1) * P], ident)
                last.then_inc(turned, 1)

            def values(u):
                t, g = units[u]
                pe.wait_ge(pt_kept, u + 1)
                if u >= 2:
                    pe.wait_ge(o_kept, u - 1)
                if t == ST and g == 2:
                    pe.wait_ge(vm_in, 16 * DB)
                pt = PTs[:, u % 2, :]
                for j in range(4):
                    r = slice((g % 2) * HD, (g % 2 + 1) * HD) if g < 2 else slice(0, P)
                    o = ps[r, 6 + u % 2, j * P:(j + 1) * P]
                    p = [pt[:, (2 * j + k) * P:(2 * j + k + 1) * P] for k in range(2)]
                    if t < ST:
                        for k in range(2):
                            val = vw[:, t + k, r] if g < 2 else mv[:, k, j * P:(j + 1) * P]
                            last = nc.tensor.matmul(o, val, p[k], start=(k == 0), stop=(k == 1))
                    elif g < 2:
                        nc.tensor.matmul(o, vw[:, NT, r], p[1], start=True, stop=False, skip_group_check=True)
                        for b in range(DB):
                            c = slice(b * DS, (b + 1) * DS)
                            last = nc.tensor.matmul(o[:, c], vwc[:, b, r], p[0][:, c], start=False, stop=(b == DB - 1), skip_group_check=True)
                    else:
                        for b in range(DB):
                            c = slice(b * DS, (b + 1) * DS)
                            for k in range(2):
                                last = nc.tensor.matmul(o[:, c], big[:, b, (k * MH + j) * P:(k * MH + j + 1) * P], p[k][:, c],
                                                        start=(k == 0), stop=(k == 1))
                last.then_inc(pv, 1)

            for i in range(N + 3):
                if i < N:
                    scores(i)
                if 2 <= i < N + 2:
                    turn(i - 2)
                if i >= 3:
                    values(i - 3)

        @block.scalar
        def _(act):
            for b in range(DB):
                act.wait_ge(cT, b + 1)
                if b >= 2:
                    act.wait_ge(cMul, b - 1)
                nc.scalar.activation(kwcT[:, b % 2, :], ps[:, 2, 0:P], ACT.Copy)
                nc.scalar.activation(big[:, 2 + b % 2, :], ps[:, 0:2, :].rearrange("p a n -> p (a n)"), ACT.Copy).then_inc(cKept, 1)
            act.wait_ge(cMul, DB)
            nc.scalar.activation(past_m[:, :, :, :].rearrange("p k h q -> p (k h q)"), ps[:, 4:6, :].rearrange("p a n -> p (a n)"), ACT.Copy).then_inc(cOut, 1)
            nc.scalar.activation(past_w[:, :, :].rearrange("p h q -> p (h q)"), ps[:, 6:8, :].rearrange("p a n -> p (a n)"), ACT.Copy).then_inc(cOut, 1)
            for i in range(N + 2):
                if i < N:
                    t, g = units[i]
                    r = i % RL
                    act.wait_ge(negd, i + 1)
                    if i >= RL:
                        act.wait_ge(turned, i - RL + 1)
                    if g < 2:
                        src, scale = L[:, r], 1.0
                        nc.scalar.activation(mx[:, r, 4, :], mx[:, r, 3, :], ACT.Exp)
                    else:
                        src, scale = ps[:, 2 * (i % 2):2 * (i % 2) + 2, :].rearrange("p a (j k) -> p (a j) k", k=2 * P), MD ** -0.5
                    for j in range(4):
                        last = nc.scalar.activation(L[:, r, j, :], src[:, j, :], ACT.Exp, bias=mx[:, r, 1, j:j + 1], scale=scale,
                                                    accum_out=mx[:, r, 2, j:j + 1])
                    last.then_inc(exped, 1)
                if i >= 2:
                    u = i - 2
                    act.wait_ge(turned, u + 1)
                    if u >= 2:
                        act.wait_ge(pv, u - 1)
                    nc.scalar.activation(PTs[:, u % 2, :], ps[:, 4:6, :].rearrange("p a n -> p (a n)"), ACT.Copy).then_inc(pt_kept, 1)

        @block.vector
        def _(dve):
            dve.wait_ge(bias_in, 32)

            def front(u):
                t, g = units[u]
                r = u % RL
                dve.wait_ge(logits, u + 1)
                if u >= RL:
                    dve.wait_ge(turned, u - RL + 1)
                src = ps[:, 2 * (u % 2):2 * (u % 2) + 2, :].rearrange("p a (j k) -> p (a j) k", k=2 * P)
                if g < 2:
                    nc.vector.tensor_tensor(L[:, r], src, bias[:, int(t == ST), g * GRP:(g + 1) * GRP, :], ALU.add).then_inc(biased, 1)
                    dve.wait_ge(biased, n_win[u])
                    if t == 0:
                        nc.vector.memset(L[:, r, :, 0:P], NEG).then_inc(padded, 1)
                        dve.wait_ge(padded, u + 1)
                    src = L[:, r]
                nc.vector.tensor_reduce(mx[:, r, 0, :], src, AX, ALU.max).then_inc(maxed, 1)
                dve.wait_ge(maxed, u + 1)
                if g < 2:
                    nc.vector.tensor_tensor(mx[:, r, 5, :], mx[:, r, 0, :], sink[:, g * GRP:(g + 1) * GRP], ALU.max).then_inc(sunk, 1)
                    dve.wait_ge(sunk, n_win[u])
                    nc.vector.tensor_tensor(mx[:, r, 3, :], sink[:, g * GRP:(g + 1) * GRP], mx[:, r, 5, :], ALU.subtract)
                    nc.vector.tensor_scalar(mx[:, r, 1, :], mx[:, r, 5, :], -1.0, None, ALU.mult).then_inc(negd, 1)
                else:
                    nc.vector.tensor_scalar(mx[:, r, 1, :], mx[:, r, 0, :], -(MD ** -0.5), None, ALU.mult).then_inc(negd, 1)

            def norm(u):
                t, g = units[u]
                r = u % RL
                dve.wait_ge(exped, u + 1)
                if g < 2:
                    nc.vector.tensor_tensor(mx[:, r, 6, :], mx[:, r, 2, :], mx[:, r, 4, :], ALU.add).then_inc(total, 1)
                    dve.wait_ge(total, n_win[u])
                    s = mx[:, r, 6, :]
                else:
                    s = mx[:, r, 2, :]
                nc.vector.reciprocal(mx[:, r, 7, :], s).then_inc(inv, 1)
                dve.wait_ge(inv, u + 1)
                nc.vector.tensor_tensor(L[:, r], L[:, r], mx[:, r, 7, :].unsqueeze(2).to_broadcast([P, 4, 2 * P]), ALU.mult).then_inc(normed, 1)

            def keep(u):
                t, g = units[u]
                dve.wait_ge(pv, u + 1)
                c = slice(t * P, (t + 1) * P)
                r = slice((g % 2) * HD, (g % 2 + 1) * HD) if g < 2 else slice(0, P)
                dst = qw if g < 2 else qm
                nc.vector.tensor_copy(dst[r, :, c], ps[r, 6 + u % 2, :].rearrange("p (j n) -> p j n", j=4)).then_inc(o_kept, 1)

            for i in range(N + 4):
                if i < N:
                    front(i)
                if 1 <= i < N + 1:
                    norm(i - 1)
                if i >= 4:
                    keep(i - 4)


def merge(nc, A, S, x1_dram):
    ident, ps, hT = S["const"][:, 0:P], S["ps"], S["hT"]
    oT = [S["qsbT"], S["qswT"], S["qmT"]]
    steps = [(n, b) for n in range(2) for b in range(3)]
    units = [(i, t) for i in range(6) for t in range(NT)]
    N = len(units)
    with ExitStack() as ctx:
        sb = lambda n, s: ctx.enter_context(nc.sbuf_tensor(n, s, F32))
        sem = lambda n: ctx.enter_context(nc.semaphore(n))
        mixed = sb("mixed", [P, NT, DM])
        wg = sb("wg", [P, 2, KC, HB])
        wo = sb("wo", [P, 2, 4, HB])
        bg = sb("bg", [P, 3 * DM])
        gt = sb("gt", [P, 3, HB])
        mT = [hT[:, i, 0:DM].rearrange("p (c n) -> p c n", c=KC) for i in range(2)]
        xt = [hT[:, 2 + i, 0:DM] for i in range(2)]
        bg_in = sem("bg_in")
        wg_in = [sem(f"wg_in{i}") for i in range(2)]
        gate = sem("gate")
        gbias = sem("gbias")
        sig = sem("sig")
        prod = sem("prod")
        mix = sem("mix")
        xt_in = [sem(f"xt_in{i}") for i in range(2)]
        mt_T = sem("mt_T")
        mt_kept = sem("mt_kept")
        outp = sem("outp")
        x1_ready = sem("x1_ready")
        x1_out = [sem(f"x1_out{i}") for i in range(2)]
        TILES = [A["x_prompt"][0, t * P:(t + 1) * P, :] for t in range(PT)] + [A["x_sample"].rearrange("b s d -> (b s) d")]
        w_v = A["w_in"][0].rearrange("(c p) n -> p c n", p=P)
        wout_v = A["w_out"][0].rearrange("(c p) n -> p c n", p=P)
        block = ctx.enter_context(nc.Block())

        @block.sync
        def _(sp):
            for i, (n, b) in enumerate(steps):
                if i >= 2:
                    sp.wait_ge(gate, (i - 1) * NT)
                o = GATE0 + b * DM + n * HB
                sp.dma_start(wg[:, i % 2], w_v[:, :, o:o + HB]).then_inc(wg_in[i % 2], 16)
                c = slice(n * HB, (n + 1) * HB)
                if b == 1:
                    v = A["w_o_sw"][0].rearrange("(g j d) n -> g d j n", g=KVH, j=GRP)
                    for g in range(KVH):
                        sp.dma_start(wo[g * HD:(g + 1) * HD, i % 2], v[g, :, :, c]).then_inc(wg_in[i % 2], 16)
                else:
                    v = A["w_o_sb" if b == 0 else "w_o_mem"][0].rearrange("(j p) n -> p j n", p=P)
                    for j in range(2):
                        sp.dma_start(wo[:, i % 2, 2 * j:2 * j + 2], v[:, 2 * j:2 * j + 2, c]).then_inc(wg_in[i % 2], 16)
                if i == 0:
                    sp.dma_start(bg[:, :], A["b_gate"][0:1, :].to_broadcast([P, 3 * DM])).then_inc(bg_in, 16)
            for i in range(2):
                sp.wait_ge(gate, (5 + i) * NT)
                sp.dma_start(wg[:, i], wout_v[:, :, i * HB:(i + 1) * HB]).then_inc(wg_in[i], 16)
            for t in range(NT):
                if t >= 2:
                    sp.wait_ge(x1_out[t % 2], 16 * (t // 2))
                sp.dma_start(xt[t % 2], TILES[t]).then_inc(xt_in[t % 2], 16)
                if t >= 1:
                    sp.wait_ge(x1_ready, t)
                    sp.dma_start(x1_dram[t - 1], xt[(t - 1) % 2]).then_inc(x1_out[(t - 1) % 2], 16)
            sp.wait_ge(x1_ready, NT)
            sp.dma_start(x1_dram[NT - 1], xt[(NT - 1) % 2]).then_inc(x1_out[(NT - 1) % 2], 16)
            sp.wait_ge(x1_out[0], 16 * 5)
            sp.wait_ge(x1_out[1], 16 * 4)

        @block.tensor
        def _(pe):
            for u, (i, t) in enumerate(units):
                if t == 0:
                    pe.wait_ge(wg_in[i % 2], 48 * (i // 2 + 1))
                if u >= 3:
                    pe.wait_ge(prod, u - 2)
                c = slice(t * P, (t + 1) * P)
                for k in range(KC):
                    nc.tensor.matmul(ps[:, u % 3, :], hT[:, k, c], wg[:, i % 2, k, :], start=(k == 0), stop=(k == KC - 1))
                for k in range(4):
                    last = nc.tensor.matmul(ps[:, 3 + u % 3, :], oT[steps[i][1]][:, k, c], wo[:, i % 2, k, :], start=(k == 0), stop=(k == 3))
                last.then_inc(gate, 1)
            pe.wait_ge(mix, N)

            def turn(t):
                if t >= 2:
                    pe.wait_ge(mt_kept, t - 1)
                for c in range(KC):
                    last = nc.tensor.transpose(ps[:, 4 + 2 * (t % 2) + c // 4, (c % 4) * P:(c % 4 + 1) * P], mixed[:, t, c * P:(c + 1) * P], ident)
                last.then_inc(mt_T, 1)

            turn(0)
            for t in range(NT):
                if t + 1 < NT:
                    turn(t + 1)
                pe.wait_ge(mt_kept, t + 1)
                if t == 0:
                    for i in range(2):
                        pe.wait_ge(wg_in[i], 48 * 3 + 16)
                if t >= 2:
                    pe.wait_ge(x1_ready, t - 1)
                for n in range(2):
                    for k in range(KC):
                        last = nc.tensor.matmul(ps[:, 2 * (t % 2) + n, :], mT[t % 2][:, k, :], wg[:, n, k, :], start=(k == 0), stop=(k == KC - 1))
                last.then_inc(outp, 1)

        @block.scalar
        def _(act):
            for u in range(N):
                act.wait_ge(gbias, u + 1)
                nc.scalar.activation(gt[:, u % 3, :], gt[:, u % 3, :], ACT.Sigmoid).then_inc(sig, 1)
            for t in range(NT):
                act.wait_ge(mt_T, t + 1)
                if t >= 2:
                    act.wait_ge(outp, t - 1)
                b = 4 + 2 * (t % 2)
                nc.scalar.activation(mT[t % 2], ps[:, b:b + 2, :].rearrange("p a (c n) -> p (a c) n", n=P), ACT.Copy).then_inc(mt_kept, 1)

        @block.vector
        def _(dve):
            dve.wait_ge(bg_in, 16)

            def front(u):
                i, t = units[u]
                n, b = steps[i]
                dve.wait_ge(gate, u + 1)
                if u >= 3:
                    dve.wait_ge(mix, u - 2)
                o = b * DM + n * HB
                nc.vector.tensor_tensor(gt[:, u % 3, :], ps[:, u % 3, :], bg[:, o:o + HB], ALU.add).then_inc(gbias, 1)

            def back(u):
                i, t = units[u]
                n, b = steps[i]
                m = mixed[:, t, n * HB:(n + 1) * HB]
                dve.wait_ge(sig, u + 1)
                dst = m if b == 0 else gt[:, u % 3, :]
                nc.vector.tensor_tensor(dst, gt[:, u % 3, :], ps[:, 3 + u % 3, :], ALU.mult).then_inc(prod, 1)
                dve.wait_ge(prod, u + 1)
                if b == 0:
                    dve.sem_inc(mix, 1)
                else:
                    nc.vector.tensor_tensor(m, m, gt[:, u % 3, :], ALU.add).then_inc(mix, 1)

            for u in range(N):
                front(u)
                if u >= 1:
                    back(u - 1)
            back(N - 1)
            for t in range(NT):
                dve.wait_ge(outp, t + 1)
                dve.wait_ge(xt_in[t % 2], 16 * (t // 2 + 1))
                b = 2 * (t % 2)
                nc.vector.tensor_tensor(xt[t % 2], xt[t % 2], ps[:, b:b + 2, :].rearrange("p a n -> p (a n)"), ALU.add).then_inc(x1_ready, 1)


GROUPS = 16
GS = SLOTS // GROUPS


def peer(nc, A, S, x1_dram):
    ident, ps = S["const"][:, 0:P], S["ps"]
    iota = S["const"][:, 5 * P:5 * P + TOPK]
    with ExitStack() as ctx:
        sb = lambda n, s, dt=F32: ctx.enter_context(nc.sbuf_tensor(n, s, dt))
        sem = lambda n: ctx.enter_context(nc.semaphore(n))
        wq = sb("wq", [P, KC, 2 * PH * P])
        keysT = sb("keysT", [P, 2 * PH, P])
        ring = sb("ring", [P, RING, 2 * DM])
        gffn = sb("gffn", [P, DM])
        x1n = sb("x1n", [P, DM])
        x1c = sb("x1c", [P, DM])
        xn = sb("xn", [P, DM])
        xnT = sb("xnT", [P, KC, P])
        qT = sb("qT", [P, 2 * PH, P])
        s = sb("s", [P, 2 * PH * NK])
        yout = sb("yout", [P, DM])
        rep = sb("rep", [P, TOPK * TOPK])
        rep2 = sb("rep2", [P, TOPK * TOPK])
        cand = sb("cand", [P, TOPK * TOPK])
        hot = sb("hot", [P, 2, TOPK, TOPK])
        v16 = sb("v16", [P, 2, TOPK])
        i16 = sb("i16", [P, 2, TOPK], U32)
        i16f = sb("i16f", [P, 2, TOPK])
        flat = sb("flat", [P, TOPK], U32)
        part = sb("part", [P, 2, TOPK], U32)
        partf = sb("partf", [P, 2, TOPK])
        e12 = sb("e12", [P, 2, TOPK])
        best = sb("best", [P, PH, TOPK])
        bsum = sb("bsum", [P, 2, PH])
        nrm = sb("p_nrm", [P, 4])
        idxn = sb("idxn", [P, SLOTS], U32)
        idx = sb("idx", [P, SLOTS], U32)
        gwn = sb("gwn", [P, SLOTS])
        gw = sb("gw", [P, SLOTS])
        hid = sb("hid", [P, SLOTS])
        act_ = sb("act_", [P, SLOTS])
        wgt = sb("wgt", [P, SLOTS])
        diag = sb("diag", [P, 2 * BATCH, P])

        wq_in = sem("wq_in")
        keys_in = sem("keys_in")
        gffn_in = sem("gffn_in")
        keys_T = sem("keys_T")
        keys_kept = sem("keys_kept")
        ring_in = [sem(f"ring_in{r}") for r in range(RING)]
        slot_free = sem("slot_free")
        issued = sem("issued")
        idx_taken = sem("idx_taken")
        tile_begun = sem("tile_begun")
        copies = sem("copies")
        dots = sem("dots")
        gelus = sem("gelus")
        weights = sem("weights")
        diags = sem("diags")
        batch_done = sem("batch_done")
        y_ready = sem("y_ready")
        y_out = sem("y_out")
        y_free = sem("y_free")
        x1n_in = sem("x1n_in")
        p_sq = sem("p_sq")
        p_ms = sem("p_ms")
        p_rt = sem("p_rt")
        acc_free = sem("acc_free")
        p_xn = sem("p_xn")
        p_xT = sem("p_xT")
        p_xkept = sem("p_xkept")
        p_q = sem("p_q")
        p_qkept = sem("p_qkept")
        p_s = sem("p_s")
        p_skept = sem("p_skept")
        p_shift = sem("p_shift")
        p_exp = sem("p_exp")
        link_ = sem("link_")
        prepared = sem("prepared")
        pool_turn = sem("pool_turn")
        dve_turn = sem("dve_turn")

        NB = SLOTS // BATCH
        acc = ps[:, 2:4, :]
        xp = ps[:, 0:2, :].rearrange("p a n -> p (a n)")
        y_v = A["y_prompt"][0].rearrange("(t p) n -> t p n", p=P)
        block = ctx.enter_context(nc.Block())

        @block.sync
        def _(sp):
            sp.dma_start(x1n[:, :], x1_dram[0]).then_inc(x1n_in, 16)
            sp.dma_start(gffn[:, :], A["norm_ffn"][0:1, :].to_broadcast([P, DM])).then_inc(gffn_in, 16)
            sp.dma_start(ring[:, 0, :].rearrange("p (a d) -> p a d", d=P), A["peer_keys"][0].rearrange("h a k d -> k (h a) d")).then_inc(keys_in, 16)
            sp.dma_start(wq[:, :, :], A["w_peer_q"][0].rearrange("(c p) n -> p c n", p=P)).then_inc(wq_in, 16)
            sp.sem_inc(y_free, 1)

            def tile(m, last):
                if not last:
                    sp.wait_ge(tile_begun, m + 1)
                    sp.dma_start(x1n[:, :], x1_dram[m + 1]).then_inc(x1n_in, 16)
                sp.wait_ge(y_ready, m + 1)
                dst = A["y_sample"].rearrange("b s n -> (b s) n") if last else y_v[m]
                sp.dma_start(dst, yout[:, :]).then_inc(y_out, 16)
                sp.wait_ge(y_out, 16 * m + 16)
                sp.sem_inc(y_free, 1)

            with sp.Fori(0, PT) as m:
                tile(m, False)
            tile(ST, True)

        @block.gpsimd
        def _(pool):
            def tile(m, last):
                pool.wait_ge(prepared, m + 1)
                pool.sem_inc(pool_turn, 1)
                nc.gpsimd.tensor_copy(idx[:, :], idxn[:, :]).then_inc(idx_taken, 1)
                pool.wait_ge(idx_taken, m + 1)
                for j in range(SLOTS):
                    pool.wait_ge(slot_free, m * SLOTS + j + 1)
                    pool.sem_inc(pool_turn, 1)
                    i = nc.gpsimd.indirect_dma_start(out=ring[:, j % RING, :], out_offset=None, in_=A["experts"],
                                                     in_offset=bass.IndirectOffsetOnAxis(ap=idx[:, j:j + 1], axis=0))
                    i.then_inc(ring_in[j % RING], 16)
                for r in range(RING):
                    pool.wait_ge(ring_in[r], (m + 1) * (16 * SLOTS // RING))

            with pool.Fori(0, PT) as m:
                tile(m, False)
            tile(ST, True)

        @block.tensor
        def _(pe):
            pe.sem_inc(slot_free, RING)
            pe.wait_ge(keys_in, 16)
            for a in range(2 * PH):
                last = nc.tensor.transpose(ps[:, 4 + a // 4, (a % 4) * P:(a % 4 + 1) * P], ring[:, 0, a * P:(a + 1) * P], ident)
            last.then_inc(keys_T, 1)
            pe.wait_ge(keys_kept, 1)
            pe.wait_ge(wq_in, 16)

            def prepare(n, g):
                if g == 2:
                    pe.wait_ge(p_xn, n + 1)
                    for c in range(KC):
                        last = nc.tensor.transpose(ps[:, 4 + c // 4, (c % 4) * P:(c % 4 + 1) * P], xn[:, c * P:(c + 1) * P], ident)
                    last.then_inc(p_xT, 1)
                if 3 <= g < 7:
                    pe.wait_ge(p_xkept, n + 1)
                    if g >= 5:
                        pe.wait_ge(p_qkept, n * 4 + g - 4)
                    for a in range(4):
                        for k in range(KC):
                            o = ((g - 3) * 4 + a) * P
                            last = nc.tensor.matmul(ps[:, 4 + g % 2, a * P:(a + 1) * P], wq[:, k, o:o + P], xnT[:, k, :],
                                                    start=(k == 0), stop=(k == KC - 1))
                    last.then_inc(p_q, 1)
                if g == 7:
                    pe.wait_ge(p_qkept, n * 4 + 4)
                    for a in range(2 * PH):
                        last = nc.tensor.matmul(ps[:, 4 + a // 4, (a % 4) * P:(a % 4 + 1) * P], qT[:, a, :], keysT[:, a, :], start=True, stop=True)
                    last.then_inc(p_s, 1)

            def tile(m, last_tile):
                for q in range(NB):
                    pe.wait_ge(diags, m * NB + q + 1)
                    if q == 0:
                        pe.wait_ge(acc_free, m + 1)
                    for j in range(q * BATCH, (q + 1) * BATCH):
                        for h in range(2):
                            last = nc.tensor.matmul(acc[:, h, :], diag[:, j % (2 * BATCH), :], ring[:, j % RING, DM + h * HB:DM + (h + 1) * HB],
                                                    start=(j == 0), stop=(j == SLOTS - 1), skip_group_check=True)
                        last.then_inc(slot_free, 1)
                    if q % 2 and not last_tile:
                        prepare(m + 1, q // 2)

            for g in range(GROUPS):
                prepare(0, g)
            with pe.Fori(0, PT) as m:
                tile(m, False)
            tile(ST, True)

        @block.scalar
        def _(act):
            act.wait_ge(keys_T, 1)
            nc.scalar.activation(keysT[:, :, :].rearrange("p a n -> p (a n)"), ps[:, 4:8, :].rearrange("p a n -> p (a n)"), ACT.Copy).then_inc(keys_kept, 1)

            def prepare(n, g):
                if g == 0:
                    act.wait_ge(x1n_in, 16 * n + 16)
                    nc.scalar.activation(qT[:, 0:KC, :].rearrange("p a n -> p (a n)"), x1n[:, :], ACT.Square, accum_out=nrm[:, 0:1]).then_inc(p_sq, 1)
                    act.wait_ge(p_ms, n + 1)
                    nc.scalar.activation(nrm[:, 2:3], nrm[:, 1:2], ACT.Sqrt).then_inc(p_rt, 1)
                if g == 2:
                    act.wait_ge(p_xT, n + 1)
                    nc.scalar.activation(xnT[:, :, :], ps[:, 4:6, :].rearrange("p a (c n) -> p (a c) n", n=P), ACT.Copy).then_inc(p_xkept, 1)
                if 3 <= g < 7:
                    act.wait_ge(p_q, n * 4 + g - 2)
                    nc.scalar.activation(qT[:, (g - 3) * 4:(g - 2) * 4, :], ps[:, 4 + g % 2, :].rearrange("p (a n) -> p a n", n=P), ACT.Copy).then_inc(p_qkept, 1)
                if g == 7:
                    act.wait_ge(p_s, n + 1)
                    nc.scalar.activation(s[:, :], ps[:, 4:8, :].rearrange("p a n -> p (a n)"), ACT.Copy).then_inc(p_skept, 1)
                if g == GROUPS - 1:
                    act.wait_ge(p_shift, n + 1)
                    nc.scalar.activation(best[:, :, :], best[:, :, :], ACT.Exp).then_inc(p_exp, 1)

            def tile(m, last_tile):
                for q in range(NB):
                    c = slice(q * BATCH, (q + 1) * BATCH)
                    act.wait_ge(dots, m * NB + q + 1)
                    nc.scalar.activation(act_[:, c], hid[:, c], ACT.Gelu_apprx_tanh).then_inc(gelus, 1)
                    act.wait_ge(weights, m * NB + q + 1)
                    if q >= 2:
                        act.wait_ge(slot_free, m * SLOTS + RING + (q - 1) * BATCH)
                    else:
                        act.wait_ge(slot_free, m * SLOTS + RING - (2 - q) * BATCH + BATCH)
                    for j in range(q * BATCH, (q + 1) * BATCH):
                        last = nc.scalar.activation(diag[:, j % (2 * BATCH), :], ident, ACT.Copy, scale=wgt[:, j:j + 1])
                    last.then_inc(diags, 1)
                    if q % 2 and not last_tile:
                        prepare(m + 1, q // 2)

            for g in range(GROUPS):
                prepare(0, g)
            with act.Fori(0, PT) as m:
                tile(m, False)
            tile(ST, True)

        @block.vector
        def _(dve):
            dve.wait_ge(gffn_in, 16)
            linked = [0]

            def prepare(n, g):
                def link(ins):
                    linked[0] += 1
                    ins.then_inc(link_, 1)
                    dve.wait_ge(link_, linked[0])

                if g == 0:
                    linked[0] = 0
                    dve.sem_clear(link_)
                    dve.wait_ge(p_sq, n + 1)
                    nc.vector.tensor_scalar(nrm[:, 1:2], nrm[:, 0:1], 1.0 / DM, EPS, ALU.mult, ALU.add).then_inc(p_ms, 1)
                if g == 1:
                    dve.wait_ge(p_rt, n + 1)
                    link(nc.vector.reciprocal(nrm[:, 3:4], nrm[:, 2:3]))
                    nc.vector.scalar_tensor_tensor(out=xn[:, :], in0=x1n[:, :], scalar=nrm[:, 3:4], in1=gffn[:, :],
                                                   op0=ALU.mult, op1=ALU.mult).then_inc(p_xn, 1)
                if g == 7:
                    dve.wait_ge(p_skept, n + 1)
                if g >= 8:
                    h = g - 8
                    for p in range(2):
                        sv = s[:, (2 * h + p) * NK:(2 * h + p + 1) * NK]
                        link(nc.vector.max(v16[:, p, 0:8], sv))
                        nc.vector.max_index(i16[:, p, 0:8], v16[:, p, 0:8], sv)
                        link(nc.vector.match_replace(rep[:, 0:NK], v16[:, p, 0:8], sv, -3.0e38))
                        link(nc.vector.max(v16[:, p, 8:16], rep[:, 0:NK]))
                        link(nc.vector.max_index(i16[:, p, 8:16], v16[:, p, 8:16], rep[:, 0:NK]))
                    c3 = cand[:, :].rearrange("p (i j) -> p i j", i=TOPK)
                    link(nc.vector.tensor_tensor(c3, v16[:, 0, :].unsqueeze(2).to_broadcast([P, TOPK, TOPK]),
                                                 v16[:, 1, :].unsqueeze(1).to_broadcast([P, TOPK, TOPK]), ALU.add))
                    nc.vector.tensor_copy(i16f[:, :, :], i16[:, :, :])
                    link(nc.vector.max(best[:, h, 0:8], cand[:, :]))
                    nc.vector.max_index(flat[:, 0:8], best[:, h, 0:8], cand[:, :])
                    link(nc.vector.match_replace(rep2[:, :], best[:, h, 0:8], cand[:, :], -3.0e38))
                    link(nc.vector.max(best[:, h, 8:16], rep2[:, :]))
                    link(nc.vector.max_index(flat[:, 8:16], best[:, h, 8:16], rep2[:, :]))
                    link(nc.vector.tensor_scalar(part[:, 0, :], flat[:, :], 4, None, ALU.logical_shift_right))
                    link(nc.vector.tensor_scalar(part[:, 1, :], flat[:, :], 15, None, ALU.bitwise_and))
                    link(nc.vector.tensor_copy(partf[:, :, :], part[:, :, :]))
                    link(nc.vector.tensor_tensor(hot[:, :, :, :].rearrange("p a k i -> p (a k) i"),
                                                 partf[:, :, :].rearrange("p a k -> p (a k)").unsqueeze(2).to_broadcast([P, 2 * TOPK, TOPK]),
                                                 iota.unsqueeze(1).to_broadcast([P, 2 * TOPK, TOPK]), ALU.is_equal))
                    link(nc.vector.tensor_tensor(hot[:, :, :, :], hot[:, :, :, :],
                                                 i16f[:, :, :].unsqueeze(2).to_broadcast([P, 2, TOPK, TOPK]), ALU.mult))
                    link(nc.vector.tensor_reduce(e12[:, :, :].rearrange("p a k -> p (a k)"), hot[:, :, :, :].rearrange("p a k i -> p (a k) i"), AX, ALU.add))
                    link(nc.vector.scalar_tensor_tensor(out=idxn[:, h * TOPK:(h + 1) * TOPK], in0=e12[:, 0, :], scalar=float(NK), in1=e12[:, 1, :],
                                                        op0=ALU.mult, op1=ALU.add))
                if g == GROUPS - 1:
                    link(nc.vector.tensor_copy(bsum[:, 1, :], best[:, :, 0]))
                    nc.vector.tensor_tensor(best[:, :, :], best[:, :, :], bsum[:, 1, :].unsqueeze(2).to_broadcast([P, PH, TOPK]), ALU.subtract).then_inc(p_shift, 1)
                    dve.wait_ge(p_exp, n + 1)
                    link(nc.vector.tensor_reduce(bsum[:, 0, :], best[:, :, :], AX, ALU.add))
                    link(nc.vector.reciprocal(bsum[:, 1, :], bsum[:, 0, :]))
                    link(nc.vector.tensor_tensor(gwn[:, :].rearrange("p (h k) -> p h k", h=PH), best[:, :, :],
                                                 bsum[:, 1, :].unsqueeze(2).to_broadcast([P, PH, TOPK]), ALU.mult))
                    dve.sem_inc(prepared, 1)

            def tile(m, last_tile):
                nc.vector.tensor_copy(gw[:, :], gwn[:, :]).then_inc(copies, 1)
                nc.vector.tensor_copy(xp, xn[:, :]).then_inc(copies, 1)
                nc.vector.tensor_copy(x1c[:, :], x1n[:, :]).then_inc(copies, 1)
                dve.wait_ge(copies, m * 3 + 3)
                dve.sem_inc(tile_begun, 1)
                for q in range(NB):
                    for j in range(q * BATCH, (q + 1) * BATCH):
                        dve.wait_ge(ring_in[j % RING], m * (16 * SLOTS // RING) + 16 * (j // RING + 1))
                        u = ring[:, j % RING, 0:DM]
                        last = nc.vector.tensor_tensor_reduce(out=u, in0=u, in1=xp, scale=1.0, scalar=0.0, op0=ALU.mult, op1=ALU.add,
                                                              accum_out=hid[:, j:j + 1])
                    last.then_inc(dots, 1)
                    dve.wait_ge(gelus, m * NB + q + 1)
                    c = slice(q * BATCH, (q + 1) * BATCH)
                    nc.vector.tensor_tensor(wgt[:, c], act_[:, c], gw[:, c], ALU.mult).then_inc(weights, 1)
                    if q % 2 and not last_tile:
                        if q == 2 * 8 + 1:
                            dve.wait_ge(idx_taken, m + 1)
                            dve.sem_inc(dve_turn, 1)
                        prepare(m + 1, q // 2)
                dve.wait_ge(slot_free, m * SLOTS + RING + SLOTS)
                dve.wait_ge(y_free, m + 1)
                nc.vector.tensor_tensor(yout[:, :], x1c[:, :], acc.rearrange("p a n -> p (a n)"), ALU.add).then_inc(y_ready, 1)
                dve.wait_ge(y_ready, m + 1)
                dve.sem_inc(acc_free, 1)

            dve.sem_inc(acc_free, 1)
            for g in range(GROUPS):
                prepare(0, g)
            with dve.Fori(0, PT) as m:
                tile(m, False)
            tile(ST, True)


def build(nc, A, small_dram, wide_dram):
    with ExitStack() as top:
        S = {}
        S["const"] = top.enter_context(nc.sbuf_tensor("const", [P, CW], F32))
        S["ps"] = top.enter_context(nc.psum_tensor("ps", [P, 8, HB], F32))
        x1_dram = nc.dram_tensor("x1_scratch", (NT, P, DM), F32, kind="Internal").ap()

        def hold(stack, name, shape):
            S[name] = stack.enter_context(nc.sbuf_tensor(name, shape, F32))

        with ExitStack() as tokens:
            hold(tokens, "hT", [P, KC, TOK])
            for n in ("qsbT", "qswT", "qmT"):
                hold(tokens, n, [P, 4, TOK])
            with ExitStack() as kv:
                hold(kv, "kswT", [P, (NT + 1) * P])
                hold(kv, "vsw", [P, NT + 1, P])
                hold(kv, "mkT", [P, MH, MT])
                hold(kv, "mv", [P, 2, MH * MD])
                with ExitStack() as sbkv:
                    hold(sbkv, "ksbT", [P, 4, TOK])
                    hold(sbkv, "vsb", [P, NT, SB_W])
                    with ExitStack() as first:
                        hold(first, "mhT", [P, KC, MT])
                        project(nc, A, S, small_dram)
                    stick(nc, A, S)
                windows(nc, A, S, wide_dram)
            merge(nc, A, S, x1_dram)
        peer(nc, A, S, x1_dram)


_INS = ["x_prompt", "mem_prompt", "x_sample", "cache_sb_k", "cache_sb_v", "cache_swa_k", "cache_swa_v",
        "cache_mem_k", "cache_mem_v", "norm_mix", "w_in", "b_gate", "q_norm_sw", "k_norm_sw", "sinks", "norm_mem",
        "w_mem_kv", "q_norm_mem", "k_norm_mem", "w_o_sb", "w_o_sw", "w_o_mem", "w_out", "norm_ffn", "w_peer_q",
        "peer_keys"]
_OUTS = {"y_prompt": (1, 1024, 1024), "y_sample": (8, 16, 1024),
         "new_sb_k_prompt": (1, 1, 1024, 8, 64), "new_sb_v_prompt": (1, 1, 1024, 8, 64),
         "new_swa_k_prompt": (1, 1, 128, 2, 64), "new_swa_v_prompt": (1, 1, 128, 2, 64),
         "new_mem_k_prompt": (1, 1, 256, 4, 128), "new_mem_v_prompt": (1, 1, 256, 4, 128),
         "new_sb_k_sample": (1, 8, 16, 8, 64), "new_sb_v_sample": (1, 8, 16, 8, 64),
         "new_swa_k_sample": (1, 8, 128, 2, 64), "new_swa_v_sample": (1, 8, 128, 2, 64)}


def kernel(**inputs):
    import numpy as _np
    import concourse.bacc as _bacc
    from concourse import mybir as _mybir
    from concourse.bass_utils import run_bass_kernel_spmd as _run

    nc = _bacc.Bacc("TRN2", target_bir_lowering=False, num_devices=1)
    arrays, A = {}, {}

    def give(name, a):
        a = _np.ascontiguousarray(a)
        arrays[f"in_{name}_dram"] = a
        return nc.dram_tensor(f"in_{name}_dram", a.shape, _mybir.dt.from_np(a.dtype), kind="ExternalInput").ap()

    for name in _INS:
        A[name] = give(name, inputs[name])
    A["experts"] = give("experts", _np.concatenate([_np.asarray(inputs["peer_u"][0]), _np.asarray(inputs["peer_v"][0])], axis=1))
    small, wide = host_constants()
    small_dram, wide_dram = give("small", small), give("wide", wide)
    for name, shape in _OUTS.items():
        A[name] = nc.dram_tensor(f"out_{name}", shape, _mybir.dt.from_np(_np.dtype("float32")), kind="ExternalOutput").ap()
    build(nc, A, small_dram, wide_dram)
    r = _run(nc, [arrays], core_ids=[0])
    return tuple(r.results[0][f"out_{name}"] for name in _OUTS)
```

```python
from contextlib import ExitStack

import numpy as np

import concourse.bass as bass
from concourse import mybir

ALU = mybir.AluOpType
ACT = mybir.ActivationFunctionType
F32 = mybir.dt.float32
U32 = mybir.dt.uint32
AX = mybir.AxisListType.X

P = 128
DM = 1024
KC = DM // P
PT = 8
ST = PT
NT = PT + 1
TOK = NT * P
DB, DS = 8, 16
HD = 64
MH, MD, MT = 4, 128, 256
SBH, SWH, KVH = 8, 8, 2
GRP = SWH // KVH
SB_W = SBH * HD
GATE0 = 2816
EPS = 1e-6
NEG = -1e30
PH, NK, TOPK = 8, 128, 16
HB = 512
SLOTS = PH * TOPK
RING = 8
BATCH = 4


def host_constants():
    i = np.arange(P)
    k, q = i[:, None], i[None, :]
    ident = np.eye(P)
    tri = -(k >= q).astype(float)
    negones = -np.ones((P, P))
    mask_p = (k < q).astype(float)
    mask_s = ((k // DS == q // DS) & (k < q)).astype(float)
    slopes = 2.0 ** (-8.0 * np.arange(1, SWH + 1) / SWH)
    qn, kn = i[:, None], np.arange(2 * P)[None, :]
    dist = np.abs(qn - kn + P)
    dchunk = (qn + P) // HD - kn // HD
    ok_p = (dchunk >= 0) & (dchunk <= 2)
    dist_s = np.where(kn < P, np.abs(P + qn % DS - kn), np.abs(qn - (kn - P)))
    ok_s = (kn < P) | ((kn - P) // DS == qn // DS)
    def bias(d, ok):
        return np.where(ok[:, None], -slopes[None, :, None] * d[:, None], NEG).reshape(P, -1)
    iota = np.tile(np.arange(TOPK), (P, 1))
    small = np.concatenate([ident, tri, negones, mask_p, mask_s, iota], axis=1).astype(np.float32)
    wide = np.concatenate([bias(dist, ok_p), bias(dist_s, ok_s)], axis=1).astype(np.float32)
    return small, wide


CW = 5 * P + TOPK
WQ = 2 * PH * P
BW = SWH * 2 * P


def project(nc, A, S, small_dram):
    ident = S["const"][:, 0:P]
    hT, mhT, ps = S["hT"], S["mhT"], S["ps"]
    with ExitStack() as ctx:
        sb = lambda n, s, dt=F32: ctx.enter_context(nc.sbuf_tensor(n, s, dt))
        sem = lambda n: ctx.enter_context(nc.semaphore(n))
        stage = sb("stage", [P, 4, HB])
        w = sb("w_qkv", [P, 2, KC, HB])
        gmix = sb("gmix", [P, 2, KC])
        gq = sb("gq_heads", [P, 2 * HD + 2 * MD])
        ss = sb("ss", [P, 3])
        nrm = sb("nrm", [P, 3, 8])
        XR = 4
        xt = [S["vsb"][:, 2 * i:2 * i + 2, :].rearrange("p a n -> p (a n)") for i in range(XR)]
        sqt = stage[:, 3, :]

        const_in = sem("const_in")
        gains_in = sem("gains_in")
        x_in = [sem(f"x_in{i}") for i in range(XR)]
        w_in = [sem(f"w_in{i}") for i in range(2)]
        x_sq = sem("x_sq")
        x_ms = sem("x_ms")
        x_rt = sem("x_rt")
        x_rs = sem("x_rs")
        x_nat = sem("x_nat")
        x_T = sem("x_T")
        h_done = sem("h_done")
        proj = sem("proj")
        copied = sem("copied")
        squared = sem("squared")
        summed = sem("summed")
        mean = sem("mean")
        rooted = sem("rooted")
        inverted = sem("inverted")
        scaled = sem("scaled")
        gained = sem("gained")
        turned = sem("turned")
        kept = sem("kept")
        pad_zero = sem("pad_zero")
        nat_out = [sem(f"nat_out{i}") for i in range(3)]
        v_out = sem("v_out")
        cache_out = sem("cache_out")

        TILES = [A["x_prompt"][0, t * P:(t + 1) * P, :] for t in range(PT)]
        TILES += [A["x_sample"].rearrange("b s d -> (b s) d")]
        TILES += [A["mem_prompt"][0, t * P:(t + 1) * P, :] for t in range(2)]
        NX = len(TILES)

        w_v = A["w_in"][0].rearrange("(c p) n -> p c n", p=P)
        wm_v = A["w_mem_kv"][0].rearrange("(c p) n -> p c n", p=P)
        BLOCKS = [("ksb", w_v[:, :, 512:1024], 512, range(NT)), ("vsb", w_v[:, :, 1024:1536], 512, range(NT)),
                  ("kvsw", w_v[:, :, 2048:2304], 256, range(NT)), ("qsw", w_v[:, :, 1536:2048], 512, range(NT)),
                  ("qm", w_v[:, :, 2304:2816], 512, range(NT)), ("mk", wm_v[:, :, 0:512], 512, range(2)),
                  ("mv", wm_v[:, :, 512:1024], 512, range(2)), ("qsb", w_v[:, :, 0:512], 512, range(12))]
        units = [(c, kind, t) for c, (kind, _, _, tiles) in enumerate(BLOCKS) for t in tiles]
        n_copy, n_norm, n_turn = [], [], []
        a = b = d = 0
        slots, s = [], 0
        n_out = [0, 0, 0]
        outs_before = []
        for _, kind, t in units:
            a += kind in ("ksb", "vsb", "mv", "qsb", "kvsw")
            b += kind in ("kvsw", "qsw", "qm", "mk")
            turns = kind in ("ksb", "kvsw", "qsw", "qm", "mk")
            d += turns
            n_copy.append(a)
            n_norm.append(b)
            n_turn.append(d)
            slots.append(s % 3 if turns else None)
            outs_before.append(n_out[s % 3] if turns else 0)
            if turns:
                if kind in ("ksb", "mk"):
                    n_out[s % 3] += 1
                if kind == "kvsw" and t == PT - 1:
                    n_out[s % 3] += 1
                if kind == "kvsw" and t == ST:
                    n_out[s % 3] += DB
                s += 1
        FINAL_OUT = list(n_out)
        last_of = {c: max(u for u, x in enumerate(units) if x[0] == c) for c in range(len(BLOCKS))}
        copies = ("ksb", "vsb", "mv", "qsb", "kvsw")
        norms = ("kvsw", "qsw", "qm", "mk")
        heads = {"kvsw": (KVH, HD), "qsw": (SWH, HD), "qm": (MH, MD), "mk": (MH, MD)}
        gain_of = {"qsw": gq[:, 0:HD], "kvsw": gq[:, HD:2 * HD], "qm": gq[:, 2 * HD:2 * HD + MD],
                   "mk": gq[:, 2 * HD + MD:2 * HD + 2 * MD]}
        NPB = 3

        def bank(u):
            return u % NPB

        def turn_bank(n):
            return 3 + n % 2

        block = ctx.enter_context(nc.Block())

        @block.sync
        def _(sp):
            sp.dma_start(S["const"][:, :], small_dram[:, :]).then_inc(const_in, 16)
            with nc.allow_non_contiguous_dma(reason="gains, a few kilobytes"):
                sp.dma_start(gmix[:, 0, :], A["norm_mix"][0].rearrange("(c p) -> p c", p=P)).then_inc(gains_in, 16)
                sp.dma_start(gmix[:, 1, :], A["norm_mem"][0].rearrange("(c p) -> p c", p=P)).then_inc(gains_in, 16)
            o = 0
            for name, n in (("q_norm_sw", HD), ("k_norm_sw", HD), ("q_norm_mem", MD), ("k_norm_mem", MD)):
                sp.dma_start(gq[:, o:o + n], A[name][0:1, :].to_broadcast([P, n])).then_inc(gains_in, 16)
                o += n

            def load_w(c):
                if c >= 2:
                    sp.wait_ge(proj, last_of[c - 2] + 1)
                n = BLOCKS[c][2]
                sp.dma_start(w[:, c % 2, :, 0:n], BLOCKS[c][1]).then_inc(w_in[c % 2], 16)

            for t in range(NX):
                if t >= XR:
                    sp.wait_ge(x_T, t - XR + 1)
                sp.dma_start(xt[t % XR], TILES[t]).then_inc(x_in[t % XR], 16)
                if t in (3, 5):
                    load_w((t - 3) // 2)
            for name, c in (("new_swa_k_sample", "cache_swa_k"), ("new_swa_v_sample", "cache_swa_v")):
                sp.dma_start(A[name][0, :, 0:P - DS].rearrange("b s h d -> b (s h d)"),
                             A[c][0, :, DS:P].rearrange("b s h d -> b (s h d)")).then_inc(cache_out, 16)
            nv = 0
            at = 2
            for u, (c, kind, t) in enumerate(units):
                if at < len(BLOCKS) and at == c + 1 and t == 0 and c >= 1:
                    load_w(at)
                    at += 1
                rows = slice(t * P, (t + 1) * P)
                q = slots[u]
                if kind == "ksb":
                    sp.wait_ge(copied, n_copy[u])
                    dst = A["new_sb_k_prompt"][0, 0, rows] if t < ST else A["new_sb_k_sample"][0].rearrange("b s h d -> (b s) h d")
                    sp.dma_start(dst.rearrange("s h d -> s (h d)"), stage[:, q, :]).then_inc(nat_out[q], 16)
                if kind == "vsb":
                    sp.wait_ge(copied, n_copy[u])
                    dst = A["new_sb_v_prompt"][0, 0, rows] if t < ST else A["new_sb_v_sample"][0].rearrange("b s h d -> (b s) h d")
                    sp.dma_start(dst.rearrange("s h d -> s (h d)"), S["vsb"][:, t, :]).then_inc(v_out, 16)
                    nv += 1
                if kind == "mk":
                    sp.wait_ge(gained, n_norm[u])
                    sp.dma_start(A["new_mem_k_prompt"][0, 0, rows].rearrange("s h d -> s (h d)"), stage[:, q, :]).then_inc(nat_out[q], 16)
                if kind == "mv":
                    sp.wait_ge(copied, n_copy[u])
                    sp.dma_start(A["new_mem_v_prompt"][0, 0, rows].rearrange("s h d -> s (h d)"), S["mv"][:, t, :]).then_inc(v_out, 16)
                    nv += 1
                if kind == "kvsw" and t == PT - 1:
                    sp.wait_ge(gained, n_norm[u])
                    sp.dma_start(A["new_swa_k_prompt"][0, 0].rearrange("s h d -> s (h d)"), stage[:, q, 0:P]).then_inc(nat_out[q], 16)
                    sp.wait_ge(copied, n_copy[u])
                    sp.dma_start(A["new_swa_v_prompt"][0, 0].rearrange("s h d -> s (h d)"), S["vsw"][:, t + 1, :]).then_inc(v_out, 16)
                    nv += 1
                if kind == "kvsw" and t == ST:
                    sp.wait_ge(gained, n_norm[u])
                    sp.wait_ge(copied, n_copy[u])
                    for b in range(DB):
                        r = slice(b * DS, (b + 1) * DS)
                        sp.dma_start(A["new_swa_k_sample"][0, b, P - DS:P].rearrange("s h d -> s (h d)"), stage[r, q, 0:P]).then_inc(nat_out[q], 16)
                        sp.dma_start(A["new_swa_v_sample"][0, b, P - DS:P].rearrange("s h d -> s (h d)"), S["vsw"][r, t + 1, :]).then_inc(v_out, 16)
                        nv += 1
            for q in range(3):
                sp.wait_ge(nat_out[q], 16 * FINAL_OUT[q])
            sp.wait_ge(v_out, 16 * nv)
            sp.wait_ge(cache_out, 32)

        @block.gpsimd
        def _(pool):
            nc.gpsimd.memset(S["kswT"][:, 0:P], 0.0).then_inc(pad_zero, 1)
            nc.gpsimd.memset(S["vsw"][:, 0, :], 0.0).then_inc(pad_zero, 1)
            pool.wait_ge(pad_zero, 2)

        @block.tensor
        def _(pe):
            pe.wait_ge(const_in, 16)
            for t in range(NX):
                pe.wait_ge(x_nat, t + 1)
                if t >= 2:
                    pe.wait_ge(h_done, t - 1)
                for c in range(KC):
                    last = nc.tensor.transpose(ps[:, 4 + 2 * (t % 2) + c // 4, (c % 4) * P:(c % 4 + 1) * P],
                                               xt[t % XR][:, c * P:(c + 1) * P], ident)
                last.then_inc(x_T, 1)
            pe.wait_ge(h_done, NX)

            def turn(u):
                c, kind, t = units[u]
                if slots[u] is None:
                    return
                n = n_turn[u] - 1
                if n >= 2:
                    pe.wait_ge(kept, n - 1)
                if kind == "ksb":
                    pe.wait_ge(copied, n_copy[u])
                else:
                    pe.wait_ge(gained, n_norm[u])
                m = 1 if kind == "kvsw" else 4
                for j in range(m):
                    last = nc.tensor.transpose(ps[:, turn_bank(n), j * P:(j + 1) * P], stage[:, slots[u], j * P:(j + 1) * P], ident)
                last.then_inc(turned, 1)

            for u, (c, kind, t) in enumerate(units):
                if t == 0:
                    pe.wait_ge(w_in[c % 2], 16 * (c // 2 + 1))
                if u >= NPB:
                    if units[u - NPB][1] in copies:
                        pe.wait_ge(copied, n_copy[u - NPB])
                    if units[u - NPB][1] in norms:
                        pe.wait_ge(scaled, n_norm[u - NPB])
                for k in range(KC):
                    if kind == "qsb":
                        j, g = t // 3, t % 3
                        last = nc.tensor.matmul(ps[:, bank(u), 0:3 * P], w[:, c % 2, k, j * P:(j + 1) * P],
                                                hT[:, k, g * 3 * P:(g + 1) * 3 * P], start=(k == 0), stop=(k == KC - 1))
                    else:
                        n = BLOCKS[c][2]
                        src = mhT if kind in ("mk", "mv") else hT
                        last = nc.tensor.matmul(ps[:, bank(u), 0:n], src[:, k, t * P:(t + 1) * P], w[:, c % 2, k, 0:n],
                                                start=(k == 0), stop=(k == KC - 1))
                last.then_inc(proj, 1)
                if u >= 2:
                    turn(u - 2)
            turn(len(units) - 2)
            turn(len(units) - 1)

        @block.scalar
        def _(act):
            for t in range(NX):
                act.wait_ge(x_in[t % XR], 16 * (t // XR + 1))
                if t >= 1:
                    act.wait_ge(x_sq, t)
                nc.scalar.activation(ps[:, 0:2, :].rearrange("p a n -> p (a n)"), xt[t % XR], ACT.Square,
                                     accum_out=ss[:, 0:1]).then_inc(x_sq, 1)
                act.wait_ge(x_ms, t + 1)
                nc.scalar.activation(ss[:, 2:3], ss[:, 1:2], ACT.Sqrt).then_inc(x_rt, 1)
            act.wait_ge(pad_zero, 2)

            def keep(u):
                c, kind, t = units[u]
                if slots[u] is None:
                    return
                act.wait_ge(turned, n_turn[u])
                src = ps[:, turn_bank(n_turn[u] - 1), :].rearrange("p (j n) -> p j n", j=4)
                cols = slice(t * P, (t + 1) * P)
                if kind == "ksb":
                    i = nc.scalar.activation(S["ksbT"][:, :, cols], src, ACT.Copy)
                elif kind == "kvsw":
                    i = nc.scalar.activation(S["kswT"][:, (t + 1) * P:(t + 2) * P], src[:, 0, :], ACT.Copy)
                elif kind == "qsw":
                    i = nc.scalar.activation(S["qswT"][:, :, cols], src, ACT.Copy, scale=HD ** -0.5)
                elif kind == "qm":
                    i = nc.scalar.activation(S["qmT"][:, :, cols], src, ACT.Copy)
                else:
                    i = nc.scalar.activation(S["mkT"][:, :, cols], src, ACT.Copy)
                i.then_inc(kept, 1)

            for u, (c, kind, t) in enumerate(units):
                act.wait_ge(proj, u + 1)
                src = ps[:, bank(u), :]
                if kind in norms:
                    H, D = heads[kind]
                    if n_norm[u] > 1:
                        act.wait_ge(summed, n_norm[u] - 1)
                    nc.scalar.activation(sqt[:, 0:H * D], src[:, 0:H * D], ACT.Square).then_inc(squared, 1)
                if kind in copies:
                    if kind == "ksb":
                        if n_turn[u] > 3:
                            act.wait_ge(turned, n_turn[u] - 3)
                            act.wait_ge(nat_out[slots[u]], 16 * outs_before[u])
                        i = nc.scalar.activation(stage[:, slots[u], :], src, ACT.Copy)
                    elif kind == "vsb":
                        i = nc.scalar.activation(S["vsb"][:, t, :], src, ACT.Copy)
                    elif kind == "mv":
                        i = nc.scalar.activation(S["mv"][:, t, :], src, ACT.Copy)
                    elif kind == "kvsw":
                        i = nc.scalar.activation(S["vsw"][:, t + 1, :], src[:, P:2 * P], ACT.Copy)
                    else:
                        j, g = t // 3, t % 3
                        i = nc.scalar.activation(S["qsbT"][:, j, g * 3 * P:(g + 1) * 3 * P], src[:, 0:3 * P], ACT.Copy, scale=HD ** -0.5)
                    i.then_inc(copied, 1)
                if kind in norms:
                    act.wait_ge(mean, n_norm[u])
                    H, D = heads[kind]
                    nc.scalar.activation(nrm[:, 1, 0:H], nrm[:, 0, 0:H], ACT.Sqrt).then_inc(rooted, 1)
                if u >= 2:
                    keep(u - 2)
            keep(len(units) - 2)
            keep(len(units) - 1)

        @block.vector
        def _(dve):
            dve.wait_ge(gains_in, 16 * 6)
            for t in range(NX + 1):
                if t < NX:
                    dve.wait_ge(x_sq, t + 1)
                    if t >= 1:
                        dve.wait_ge(x_rt, t)
                    nc.vector.tensor_scalar(ss[:, 1:2], ss[:, 0:1], 1.0 / DM, EPS, ALU.mult, ALU.add).then_inc(x_ms, 1)
                    dve.wait_ge(x_rt, t + 1)
                    nc.vector.reciprocal(nrm[:, 2, 0:1], ss[:, 2:3]).then_inc(x_rs, 1)
                    dve.wait_ge(x_rs, t + 1)
                    nc.vector.tensor_scalar(xt[t % XR], xt[t % XR], nrm[:, 2, 0:1], None, ALU.mult).then_inc(x_nat, 1)
                if t >= 1:
                    v = t - 1
                    dve.wait_ge(x_T, v + 1)
                    b = 4 + 2 * (v % 2)
                    src = ps[:, b:b + 2, :].rearrange("p a (c n) -> p (a c) n", n=P)
                    if v < NT:
                        dst, g = hT[:, :, v * P:(v + 1) * P], gmix[:, 0, :]
                    else:
                        dst, g = mhT[:, :, (v - NT) * P:(v - NT + 1) * P], gmix[:, 1, :]
                    nc.vector.tensor_tensor(dst, src, g.unsqueeze(2).to_broadcast([P, KC, P]), ALU.mult).then_inc(h_done, 1)
            for u, (c, kind, t) in enumerate(units):
                if kind not in norms:
                    continue
                H, D = heads[kind]
                n = n_norm[u]
                dve.wait_ge(squared, n)
                if n > 1:
                    dve.wait_ge(inverted, n - 1)
                nc.vector.tensor_reduce(nrm[:, 2, 0:H], sqt[:, 0:H * D].rearrange("p (h d) -> p h d", h=H), AX, ALU.add).then_inc(summed, 1)
                dve.wait_ge(summed, n)
                nc.vector.tensor_scalar(nrm[:, 0, 0:H], nrm[:, 2, 0:H], 1.0 / D, EPS, ALU.mult, ALU.add).then_inc(mean, 1)
                dve.wait_ge(rooted, n)
                nc.vector.reciprocal(nrm[:, 2, 0:H], nrm[:, 1, 0:H]).then_inc(inverted, 1)
                dve.wait_ge(inverted, n)
                dve.wait_ge(proj, u + 1)
                if n_turn[u] > 3:
                    dve.wait_ge(turned, n_turn[u] - 3)
                    if outs_before[u]:
                        dve.wait_ge(nat_out[slots[u]], 16 * outs_before[u])
                nat = stage[:, slots[u], 0:H * D]
                if kind == "qsw":
                    out = nat.rearrange("p (j g d) -> p g j d", g=KVH, j=GRP)
                    src = ps[:, bank(u), 0:H * D].rearrange("p (g j d) -> p g j d", g=KVH, j=GRP)
                    r = nrm[:, 2, 0:H].rearrange("p (g j) -> p g j", g=KVH).unsqueeze(3).to_broadcast([P, KVH, GRP, D])
                else:
                    out = nat.rearrange("p (h d) -> p h d", h=H)
                    src = ps[:, bank(u), 0:H * D].rearrange("p (h d) -> p h d", h=H)
                    r = nrm[:, 2, 0:H].unsqueeze(2).to_broadcast([P, H, D])
                nc.vector.tensor_tensor(out, src, r, ALU.mult).then_inc(scaled, 1)
                dve.wait_ge(scaled, n)
                flat = nat.rearrange("p (h d) -> p h d", h=H)
                nc.vector.tensor_tensor(flat, flat, gain_of[kind].unsqueeze(1).to_broadcast([P, H, D]), ALU.mult).then_inc(gained, 1)


def stick(nc, A, S):
    ident, tri, negones = (S["const"][:, i * P:(i + 1) * P] for i in range(3))
    masks = [S["const"][:, 3 * P:4 * P], S["const"][:, 4 * P:5 * P]]
    qT, kT, v, ps = S["qsbT"], S["ksbT"], S["vsb"], S["ps"]
    steps = [(t, kb, kb == t, kb == 0) for t in range(PT) for kb in range(t, -1, -1)]
    steps += [(ST, ST, True, False), (ST, None, False, True)]
    N = len(steps)
    W8 = SBH * P
    ZC = 5
    with ExitStack() as ctx:
        sb = lambda n, s: ctx.enter_context(nc.sbuf_tensor(n, s, F32))
        sem = lambda n: ctx.enter_context(nc.semaphore(n))
        za = sb("za", [P, 2, W8])
        zc = sb("zc", [P, ZC, W8])
        sp_ = sb("sp", [P, 2, W8])
        later = sb("later", [P, 2, W8])

        def kcache(b):
            return (za, later)[b // 4][:, b // 2 % 2, (b % 2) * SB_W:(b % 2 + 1) * SB_W]

        kcT = sb("kcT", [P, DB, 4, P])
        kc_in = [sem(f"kc_in{i}") for i in range(DB)]
        vc_in = sem("vc_in")
        kc_T = sem("kc_T")
        kc_kept = sem("kc_kept")
        logits = sem("logits")
        absd = sem("absd")
        exped = sem("exped")
        logd = sem("logd")
        zcopied = sem("zcopied")
        sp_raw = sem("sp_raw")
        sp_ready = sem("sp_ready")
        later_ready = sem("later_ready")
        sums = sem("sums")
        expo = sem("expo")
        added = sem("added")
        weight = sem("weight")
        masked = sem("masked")
        pv = sem("pv")
        o_kept = sem("o_kept")
        diag = [sum(s[2] for s in steps[:n + 1]) for n in range(N)]
        ends = [sum(s[3] for s in steps[:n + 1]) for n in range(N)]

        def vcache(b):
            return kT[:, b // 2, (b % 2) * SB_W:(b % 2 + 1) * SB_W]

        block = ctx.enter_context(nc.Block())

        @block.sync
        def _(sp):
            for b in range(DB):
                sp.dma_start(kcache(b), A["cache_sb_k"][0, b].rearrange("s h d -> s (h d)")).then_inc(kc_in[b], 16)
            sp.wait_ge(logits, N - 2)
            for b in range(DB):
                sp.dma_start(vcache(b), A["cache_sb_v"][0, b].rearrange("s h d -> s (h d)")).then_inc(vc_in, 16)

        @block.tensor
        def _(pe):
            for b in range(DB):
                pe.wait_ge(kc_in[b], 16)
                if b >= 4:
                    pe.wait_ge(kc_kept, b - 3)
                for j in range(4):
                    last = nc.tensor.transpose(ps[:, b % 4, j * P:(j + 1) * P], kcache(b)[:, j * P:(j + 1) * P], ident)
                last.then_inc(kc_T, 1)
            pe.wait_ge(kc_kept, DB)

            def score(n):
                t, kb, _, _ = steps[n]
                if n >= 2:
                    pe.wait_ge(zcopied, n - 1)
                    pe.wait_ge(sp_raw, n - 1)
                for h in range(SBH):
                    r = slice((h % 2) * HD, (h % 2 + 1) * HD)
                    o = ps[:, 2 * (n % 2) + h % 2, (h // 2) * P:(h // 2 + 1) * P]
                    if kb is not None:
                        last = nc.tensor.matmul(o, kT[r, h // 2, kb * P:(kb + 1) * P], qT[r, h // 2, t * P:(t + 1) * P],
                                                start=True, stop=True)
                        continue
                    for b in range(DB):
                        c = slice(b * DS, (b + 1) * DS)
                        last = nc.tensor.matmul(o[:, c], kcT[r, b, h // 2, :], qT[r, h // 2, t * P + b * DS:t * P + (b + 1) * DS],
                                                start=True, stop=True)
                last.then_inc(logits, 1)

            def suffix(n):
                first = steps[n][2]
                pe.wait_ge(sp_ready, n + 1)
                if n >= 1:
                    pe.wait_ge(expo, n)
                if not first:
                    pe.wait_ge(later_ready, n)
                for i in range(2):
                    last = nc.tensor.matmul(ps[:, 4 + i, :], tri, sp_[:, n % 2, i * HB:(i + 1) * HB], start=True, stop=first)
                    if not first:
                        last = nc.tensor.matmul(ps[:, 4 + i, :], negones, later[:, (n - 1) % 2, i * HB:(i + 1) * HB],
                                                start=False, stop=True)
                last.then_inc(sums, 1)

            def values(n):
                t, kb, first, end = steps[n]
                if first:
                    pe.wait_ge(masked, diag[n])
                    if t >= 2:
                        pe.wait_ge(o_kept, t - 1)
                else:
                    pe.wait_ge(weight, n + 1)
                if kb is None:
                    pe.wait_ge(vc_in, 16 * DB)
                w = zc[:, n % ZC, :]
                for h in range(SBH):
                    at = ((h % 2) * (SBH // 2) + h // 2) * P
                    o = ps[(h % 2) * HD:(h % 2 + 1) * HD, 6 + t % 2, (h // 2) * P:(h // 2 + 1) * P]
                    if kb is not None:
                        last = nc.tensor.matmul(o, v[:, kb, h * HD:(h + 1) * HD], w[:, at:at + P],
                                                start=first and h < 2, stop=end, skip_group_check=True)
                        continue
                    for b in range(DB):
                        last = nc.tensor.matmul(o[:, b * DS:(b + 1) * DS], vcache(b)[:, h * HD:(h + 1) * HD],
                                                w[:, at + b * DS:at + (b + 1) * DS], start=False, stop=True,
                                                skip_group_check=True)
                last.then_inc(pv, 1)

            score(0)
            score(1)
            for n in range(N):
                suffix(n)
                if n + 2 < N:
                    score(n + 2)
                if n >= 2:
                    values(n - 2)
            values(N - 2)
            values(N - 1)

        @block.scalar
        def _(act):
            nc.scalar.preload_act_table_set("natural_log_exp_and_others")
            for b in range(DB):
                act.wait_ge(kc_T, b + 1)
                nc.scalar.activation(kcT[:, b], ps[:, b % 4, :].rearrange("p (j n) -> p j n", j=4), ACT.Copy).then_inc(kc_kept, 1)

            def weigh(n):
                act.wait_ge(expo, n + 1)
                nc.scalar.activation(zc[:, n % ZC, :], zc[:, n % ZC, :], ACT.Exp).then_inc(weight, 1)

            for n in range(N):
                z = ps[:, 2 * (n % 2):2 * (n % 2) + 2, :].rearrange("p a n -> p (a n)")
                act.wait_ge(logits, n + 1)
                if n >= 2:
                    act.wait_ge(sp_raw, n - 1)
                if n >= ZC:
                    act.wait_ge(pv, n - ZC + 1)
                nc.scalar.activation(za[:, n % 2, :], z, ACT.Abs).then_inc(absd, 1)
                nc.scalar.activation(zc[:, n % ZC, :], z, ACT.Copy).then_inc(zcopied, 1)
                act.wait_ge(absd, n + 1)
                nc.scalar.activation(za[:, n % 2, :], za[:, n % 2, :], ACT.Exp, scale=-1.0).then_inc(exped, 1)
                act.wait_ge(exped, n + 1)
                nc.scalar.activation(za[:, n % 2, :], za[:, n % 2, :], ACT.Ln, bias=1.0).then_inc(logd, 1)
                if n >= 2:
                    weigh(n - 2)
            weigh(N - 2)
            weigh(N - 1)

        @block.gpsimd
        def _(pool):
            def later_sum(n):
                pool.wait_ge(sp_ready, n + 1)
                if n >= 2:
                    pool.wait_ge(sums, n)
                if n >= 1:
                    pool.wait_ge(later_ready, n)
                if steps[n][2]:
                    nc.gpsimd.tensor_copy(later[:, n % 2, :], sp_[:, n % 2, :]).then_inc(later_ready, 1)
                else:
                    nc.gpsimd.tensor_tensor(later[:, n % 2, :], later[:, (n - 1) % 2, :], sp_[:, n % 2, :], ALU.add).then_inc(later_ready, 1)

            def mask_weight(n):
                if steps[n][2]:
                    m = masks[steps[n][0] == ST].unsqueeze(1).to_broadcast([P, SBH, P])
                    w = zc[:, n % ZC, :].rearrange("p (h q) -> p h q", h=SBH)
                    pool.wait_ge(weight, n + 1)
                    nc.gpsimd.tensor_tensor(w, w, m, ALU.mult).then_inc(masked, 1)

            for n in range(N):
                later_sum(n)
                if n >= 2:
                    mask_weight(n - 2)
            mask_weight(N - 2)

        @block.vector
        def _(dve):
            def soft(n):
                t, _, first, _ = steps[n]
                z = ps[:, 2 * (n % 2):2 * (n % 2) + 2, :].rearrange("p a n -> p (a n)")
                s = sp_[:, n % 2, :]
                dve.wait_ge(logd, n + 1)
                if n >= 2:
                    dve.wait_ge(sums, n - 1)
                    dve.wait_ge(later_ready, n - 1)
                i = nc.vector.scalar_tensor_tensor(out=s, in0=z, scalar=0.0, in1=za[:, n % 2, :], op0=ALU.max, op1=ALU.add)
                i.then_inc(sp_raw, 1)
                dve.wait_ge(sp_raw, n + 1)
                if first:
                    m = masks[t == ST].unsqueeze(1).to_broadcast([P, SBH, P])
                    s3 = s.rearrange("p (h q) -> p h q", h=SBH)
                    nc.vector.tensor_tensor(s3, s3, m, ALU.mult).then_inc(sp_ready, 1)
                else:
                    dve.sem_inc(sp_ready, 1)

            def exponent(n):
                dve.wait_ge(sums, n + 1)
                dve.wait_ge(zcopied, n + 1)
                c = zc[:, n % ZC, :]
                nc.vector.tensor_tensor(c, c, ps[:, 4:6, :].rearrange("p a n -> p (a n)"), ALU.add).then_inc(added, 1)
                dve.wait_ge(added, n + 1)
                if steps[n][2]:
                    nc.vector.tensor_scalar(c, c, 0.0, None, ALU.min).then_inc(expo, 1)
                else:
                    dve.sem_inc(expo, 1)

            def keep(n):
                t, _, _, end = steps[n]
                if end:
                    dve.wait_ge(pv, n + 1)
                    nc.vector.tensor_copy(qT[:, :, t * P:(t + 1) * P], ps[:, 6 + t % 2, :].rearrange("p (j n) -> p j n", j=4)).then_inc(o_kept, 1)

            for n in range(N):
                soft(n)
                if n >= 1:
                    exponent(n - 1)
                if n >= 3:
                    keep(n - 3)
            exponent(N - 1)
            keep(N - 3)
            keep(N - 2)
            keep(N - 1)


def windows(nc, A, S, wide_dram):
    ident, ps = S["const"][:, 0:P], S["ps"]
    qw, kw, vw, qm, mk, mv = S["qswT"], S["kswT"], S["vsw"], S["qmT"], S["mkT"], S["mv"]
    units = [(t, g) for t in range(NT) for g in (0, 1, 2)]
    N = len(units)
    W = 4 * 2 * P
    RL = 3
    with ExitStack() as ctx:
        sb = lambda n, s: ctx.enter_context(nc.sbuf_tensor(n, s, F32))
        sem = lambda n: ctx.enter_context(nc.semaphore(n))
        bias = sb("bias", [P, 2, SWH, 2 * P])
        sink = sb("sink", [P, SWH])
        L = sb("L", [P, RL, 4, 2 * P])
        PTs = sb("PTs", [P, 2, W])
        past_w = sb("past_w", [P, SWH, P])
        past_m = sb("past_m", [P, 2, MH, P])
        kwc = sb("kwc", [P, DB, P])
        kwcT = sb("kwcT", [P, 2, P])
        vwc = sb("vwc", [P, DB, P])
        big = sb("big", [P, DB, 2 * MH * MD])
        mx = sb("mx", [P, RL, 8, 4])
        bias_in = sem("bias_in")
        kw_in = sem("kw_in")
        vw_in = sem("vw_in")
        km_in = [sem(f"km_in{i}") for i in range(2)]
        vm_in = sem("vm_in")
        cT = sem("cT")
        cKept = sem("cKept")
        cMul = sem("cMul")
        cOut = sem("cOut")
        logits = sem("w_logits")
        biased = sem("biased")
        padded = sem("padded")
        maxed = sem("maxed")
        sunk = sem("sunk")
        negd = sem("negd")
        exped = sem("w_exped")
        total = sem("total")
        inv = sem("inv")
        normed = sem("normed")
        turned = sem("w_turned")
        pt_kept = sem("pt_kept")
        pv = sem("w_pv")
        o_kept = sem("w_o_kept")
        n_win = [sum(g < 2 for _, g in units[:u + 1]) for u in range(N)]

        kview = A["cache_mem_k"][0].rearrange("b (k p) h d -> b p k (h d)", p=P)
        vview = A["cache_mem_v"][0].rearrange("b (k p) h d -> b p k (h d)", p=P)
        two = lambda x: x.rearrange("p (k n) -> p k n", k=2)
        block = ctx.enter_context(nc.Block())

        @block.sync
        def _(sp):
            sp.dma_start(kwc[:, :, :], A["cache_swa_k"][0].rearrange("b s h d -> s b (h d)")).then_inc(kw_in, 16)
            for b in range(DB):
                if b == 2:
                    sp.dma_start(bias[:, :, :, :].rearrange("p a h k -> p (a h k)"), wide_dram[:, :]).then_inc(bias_in, 16)
                    sp.dma_start(sink[:, :], A["sinks"][0:1, :].to_broadcast([P, SWH])).then_inc(bias_in, 16)
                    sp.dma_start(vwc[:, :, :], A["cache_swa_v"][0].rearrange("b s h d -> s b (h d)")).then_inc(vw_in, 16)
                if b >= 2:
                    sp.wait_ge(cT, b - 1)
                sp.dma_start(two(big[:, b % 2, :]), kview[b]).then_inc(km_in[b % 2], 16)
            sp.wait_ge(cMul, DB)
            for b in range(DB):
                sp.dma_start(two(big[:, b, :]), vview[b]).then_inc(vm_in, 16)

        @block.tensor
        def _(pe):
            def turn_keys(b):
                pe.wait_ge(km_in[b % 2], 16 * (b // 2 + 1))
                if b >= 1:
                    pe.wait_ge(cKept, b)
                for j in range(8):
                    nc.tensor.transpose(ps[:, j // 4, (j % 4) * P:(j % 4 + 1) * P], big[:, b % 2, j * P:(j + 1) * P], ident)
                nc.tensor.transpose(ps[:, 2, 0:P], kwc[:, b, :], ident).then_inc(cT, 1)

            def multiply_keys(b):
                pe.wait_ge(cKept, b + 1)
                c = slice(ST * P + b * DS, ST * P + (b + 1) * DS)
                for k in range(2):
                    for h in range(MH):
                        nc.tensor.matmul(ps[:, 4 + k, h * P + b * DS:h * P + (b + 1) * DS],
                                         big[:, 2 + b % 2, (k * MH + h) * P:(k * MH + h + 1) * P], qm[:, h, c], start=True, stop=True)
                for g in range(KVH):
                    r = slice(g * HD, (g + 1) * HD)
                    o = ps[:, 6 + g, :].rearrange("p (j q) -> p j q", j=GRP)[:, :, b * DS:(b + 1) * DS]
                    last = nc.tensor.matmul(o, kwcT[r, b % 2, :], qw[r, :, c], start=True, stop=True)
                last.then_inc(cMul, 1)

            pe.wait_ge(kw_in, 16)
            turn_keys(0)
            for b in range(DB):
                if b + 1 < DB:
                    turn_keys(b + 1)
                multiply_keys(b)
            pe.wait_ge(cOut, 2)

            def scores(u):
                t, g = units[u]
                if u >= 2:
                    pe.wait_ge(exped, u - 1)
                    pe.wait_ge(maxed, u - 1)
                o = ps[:, 2 * (u % 2):2 * (u % 2) + 2, :].rearrange("p a (j k) -> p (a j) k", k=2 * P)
                for j in range(4):
                    r = slice((g % 2) * HD, (g % 2 + 1) * HD)
                    if g < 2 and t < ST:
                        last = nc.tensor.matmul(o[:, j, :], qw[r, j, t * P:(t + 1) * P], kw[r, t * P:(t + 2) * P], start=True, stop=True)
                    elif g < 2:
                        nc.tensor.transpose(o[:, j, 0:P], past_w[:, g * GRP + j, :], ident)
                        last = nc.tensor.matmul(o[:, j, P:2 * P], qw[r, j, t * P:(t + 1) * P], kw[r, NT * P:(NT + 1) * P], start=True, stop=True)
                    elif t < ST:
                        last = nc.tensor.matmul(o[:, j, :], qm[:, j, t * P:(t + 1) * P], mk[:, j, :], start=True, stop=True)
                    else:
                        for k in range(2):
                            last = nc.tensor.transpose(o[:, j, k * P:(k + 1) * P], past_m[:, k, j, :], ident)
                last.then_inc(logits, 1)

            def turn(u):
                pe.wait_ge(normed, u + 1)
                if u >= 1:
                    pe.wait_ge(pt_kept, u)
                for i in range(8):
                    last = nc.tensor.transpose(ps[:, 4 + i // 4, (i % 4) * P:(i % 4 + 1) * P], L[:, u % RL, i // 2, (i % 2) * P:(i % 2 + 1) * P], ident)
                last.then_inc(turned, 1)

            def values(u):
                t, g = units[u]
                pe.wait_ge(pt_kept, u + 1)
                if u >= 2:
                    pe.wait_ge(o_kept, u - 1)
                if t == ST:
                    pe.wait_ge(vw_in, 16)
                if t == ST and g == 2:
                    pe.wait_ge(vm_in, 16 * DB)
                pt = PTs[:, u % 2, :]
                for j in range(4):
                    r = slice((g % 2) * HD, (g % 2 + 1) * HD) if g < 2 else slice(0, P)
                    o = ps[r, 6 + u % 2, j * P:(j + 1) * P]
                    p = [pt[:, (2 * j + k) * P:(2 * j + k + 1) * P] for k in range(2)]
                    if t < ST:
                        for k in range(2):
                            val = vw[:, t + k, r] if g < 2 else mv[:, k, j * P:(j + 1) * P]
                            last = nc.tensor.matmul(o, val, p[k], start=(k == 0), stop=(k == 1))
                    elif g < 2:
                        nc.tensor.matmul(o, vw[:, NT, r], p[1], start=(j == 0), stop=False, skip_group_check=True)
                        if j < 3:
                            continue
                        heads = lambda x: x.rearrange("p (j q) -> p j q", j=GRP)
                        past = pt.rearrange("p (j k q) -> p j k q", j=GRP, k=2)[:, :, 0, :]
                        for b in range(DB):
                            c = slice(b * DS, (b + 1) * DS)
                            last = nc.tensor.matmul(heads(ps[r, 6 + u % 2, :])[:, :, c], vwc[:, b, r], past[:, :, c],
                                                    start=False, stop=(b == DB - 1), skip_group_check=True)
                    else:
                        for b in range(DB):
                            c = slice(b * DS, (b + 1) * DS)
                            for k in range(2):
                                last = nc.tensor.matmul(o[:, c], big[:, b, (k * MH + j) * P:(k * MH + j + 1) * P], p[k][:, c],
                                                        start=(k == 0), stop=(k == 1))
                last.then_inc(pv, 1)

            for i in range(N + 3):
                if i < N:
                    scores(i)
                if 2 <= i < N + 2:
                    turn(i - 2)
                if i >= 3:
                    values(i - 3)

        @block.scalar
        def _(act):
            for b in range(DB):
                act.wait_ge(cT, b + 1)
                if b >= 2:
                    act.wait_ge(cMul, b - 1)
                nc.scalar.activation(kwcT[:, b % 2, :], ps[:, 2, 0:P], ACT.Copy)
                nc.scalar.activation(big[:, 2 + b % 2, :], ps[:, 0:2, :].rearrange("p a n -> p (a n)"), ACT.Copy).then_inc(cKept, 1)
            act.wait_ge(cMul, DB)
            nc.scalar.activation(past_m[:, :, :, :].rearrange("p k h q -> p (k h q)"), ps[:, 4:6, :].rearrange("p a n -> p (a n)"), ACT.Copy).then_inc(cOut, 1)
            nc.scalar.activation(past_w[:, :, :].rearrange("p h q -> p (h q)"), ps[:, 6:8, :].rearrange("p a n -> p (a n)"), ACT.Copy).then_inc(cOut, 1)
            for i in range(N + 2):
                if i >= 2:
                    u = i - 2
                    act.wait_ge(turned, u + 1)
                    if u >= 2:
                        act.wait_ge(pv, u - 1)
                    nc.scalar.activation(PTs[:, u % 2, :], ps[:, 4:6, :].rearrange("p a n -> p (a n)"), ACT.Copy).then_inc(pt_kept, 1)
                if i < N:
                    t, g = units[i]
                    r = i % RL
                    act.wait_ge(negd, i + 1)
                    if i >= RL:
                        act.wait_ge(turned, i - RL + 1)
                    if g < 2:
                        src, scale = L[:, r], 1.0
                        nc.scalar.activation(mx[:, r, 4, :], mx[:, r, 3, :], ACT.Exp)
                    else:
                        src, scale = ps[:, 2 * (i % 2):2 * (i % 2) + 2, :].rearrange("p a (j k) -> p (a j) k", k=2 * P), MD ** -0.5
                    for j in range(4):
                        last = nc.scalar.activation(L[:, r, j, :], src[:, j, :], ACT.Exp, bias=mx[:, r, 1, j:j + 1], scale=scale,
                                                    accum_out=mx[:, r, 2, j:j + 1])
                    last.then_inc(exped, 1)

        @block.vector
        def _(dve):
            dve.wait_ge(bias_in, 32)

            def front(u):
                t, g = units[u]
                r = u % RL
                dve.wait_ge(logits, u + 1)
                if u >= RL:
                    dve.wait_ge(turned, u - RL + 1)
                src = ps[:, 2 * (u % 2):2 * (u % 2) + 2, :].rearrange("p a (j k) -> p (a j) k", k=2 * P)
                if g < 2:
                    nc.vector.tensor_tensor(L[:, r], src, bias[:, int(t == ST), g * GRP:(g + 1) * GRP, :], ALU.add).then_inc(biased, 1)
                    dve.wait_ge(biased, n_win[u])
                    if t == 0:
                        nc.vector.memset(L[:, r, :, 0:P], NEG).then_inc(padded, 1)
                        dve.wait_ge(padded, u + 1)
                    src = L[:, r]
                nc.vector.tensor_reduce(mx[:, r, 0, :], src, AX, ALU.max).then_inc(maxed, 1)
                dve.wait_ge(maxed, u + 1)
                if g < 2:
                    nc.vector.tensor_tensor(mx[:, r, 5, :], mx[:, r, 0, :], sink[:, g * GRP:(g + 1) * GRP], ALU.max).then_inc(sunk, 1)
                    dve.wait_ge(sunk, n_win[u])
                    nc.vector.tensor_tensor(mx[:, r, 3, :], sink[:, g * GRP:(g + 1) * GRP], mx[:, r, 5, :], ALU.subtract)
                    nc.vector.tensor_scalar(mx[:, r, 1, :], mx[:, r, 5, :], -1.0, None, ALU.mult).then_inc(negd, 1)
                else:
                    nc.vector.tensor_scalar(mx[:, r, 1, :], mx[:, r, 0, :], -(MD ** -0.5), None, ALU.mult).then_inc(negd, 1)

            def norm(u):
                t, g = units[u]
                r = u % RL
                dve.wait_ge(exped, u + 1)
                if g < 2:
                    nc.vector.tensor_tensor(mx[:, r, 6, :], mx[:, r, 2, :], mx[:, r, 4, :], ALU.add).then_inc(total, 1)
                    dve.wait_ge(total, n_win[u])
                    s = mx[:, r, 6, :]
                else:
                    s = mx[:, r, 2, :]
                nc.vector.reciprocal(mx[:, r, 7, :], s).then_inc(inv, 1)
                dve.wait_ge(inv, u + 1)
                nc.vector.tensor_tensor(L[:, r], L[:, r], mx[:, r, 7, :].unsqueeze(2).to_broadcast([P, 4, 2 * P]), ALU.mult).then_inc(normed, 1)

            def keep(u):
                t, g = units[u]
                dve.wait_ge(pv, u + 1)
                c = slice(t * P, (t + 1) * P)
                r = slice((g % 2) * HD, (g % 2 + 1) * HD) if g < 2 else slice(0, P)
                dst = qw if g < 2 else qm
                nc.vector.tensor_copy(dst[r, :, c], ps[r, 6 + u % 2, :].rearrange("p (j n) -> p j n", j=4)).then_inc(o_kept, 1)

            for i in range(N + 4):
                if i < N:
                    front(i)
                if 1 <= i < N + 1:
                    norm(i - 1)
                if i >= 4:
                    keep(i - 4)


def merge(nc, A, S, x1_dram):
    ident, ps, hT = S["const"][:, 0:P], S["ps"], S["hT"]
    oT = [S["qsbT"], S["qswT"], S["qmT"]]
    steps = [(n, b) for n in range(2) for b in range(3)]
    units = [(i, t) for i in range(6) for t in range(NT)]
    N = len(units)
    with ExitStack() as ctx:
        sb = lambda n, s: ctx.enter_context(nc.sbuf_tensor(n, s, F32))
        sem = lambda n: ctx.enter_context(nc.semaphore(n))
        mixed = sb("mixed", [P, NT, DM])
        wg = sb("wg", [P, 2, KC, HB])
        wo = sb("wo", [P, 2, 4, HB])
        bg = sb("bg", [P, 3 * DM])
        gt = sb("gt", [P, 3, HB])
        mT = [hT[:, 4 + i, 0:DM].rearrange("p (c n) -> p c n", c=KC) for i in range(2)]
        xt = [hT[:, 6 + i, 0:DM] for i in range(2)]
        bg_in = sem("bg_in")
        wq_in = sem("wq_in")
        wg_in = [sem(f"wg_in{i}") for i in range(2)]
        gate = sem("gate")
        gbias = sem("gbias")
        sig = sem("sig")
        prod = sem("prod")
        mix = sem("mix")
        xt_in = [sem(f"xt_in{i}") for i in range(2)]
        mt_T = sem("mt_T")
        mt_kept = sem("mt_kept")
        outp = sem("outp")
        x1_ready = sem("x1_ready")
        x1_out = [sem(f"x1_out{i}") for i in range(2)]
        TILES = [A["x_prompt"][0, t * P:(t + 1) * P, :] for t in range(PT)] + [A["x_sample"].rearrange("b s d -> (b s) d")]
        w_v = A["w_in"][0].rearrange("(c p) n -> p c n", p=P)
        wout_v = A["w_out"][0].rearrange("(c p) n -> p c n", p=P)
        block = ctx.enter_context(nc.Block())

        @block.sync
        def _(sp):
            for i, (n, b) in enumerate(steps):
                if i >= 2:
                    sp.wait_ge(gate, (i - 1) * NT)
                o = GATE0 + b * DM + n * HB
                sp.dma_start(wg[:, i % 2], w_v[:, :, o:o + HB]).then_inc(wg_in[i % 2], 16)
                c = slice(n * HB, (n + 1) * HB)
                if b == 1:
                    v = A["w_o_sw"][0].rearrange("(g j d) n -> g d j n", g=KVH, j=GRP)
                    for g in range(KVH):
                        sp.dma_start(wo[g * HD:(g + 1) * HD, i % 2], v[g, :, :, c]).then_inc(wg_in[i % 2], 16)
                else:
                    v = A["w_o_sb" if b == 0 else "w_o_mem"][0].rearrange("(j p) n -> p j n", p=P)
                    for j in range(2):
                        sp.dma_start(wo[:, i % 2, 2 * j:2 * j + 2], v[:, 2 * j:2 * j + 2, c]).then_inc(wg_in[i % 2], 16)
                if i == 0:
                    sp.dma_start(bg[:, :], A["b_gate"][0:1, :].to_broadcast([P, 3 * DM])).then_inc(bg_in, 16)
            for i in range(2):
                sp.wait_ge(gate, (5 + i) * NT)
                sp.dma_start(wg[:, i], wout_v[:, :, i * HB:(i + 1) * HB]).then_inc(wg_in[i], 16)
            for t in range(NT):
                if t >= 2:
                    sp.wait_ge(x1_out[t % 2], 16 * (t // 2))
                sp.dma_start(xt[t % 2], TILES[t]).then_inc(xt_in[t % 2], 16)
                if t == 1:
                    sp.dma_start(S["wq"], A["w_peer_q"][0].rearrange("(c p) n -> p c n", p=P)).then_inc(wq_in, 16)
                if t >= 1:
                    sp.wait_ge(x1_ready, t)
                    sp.dma_start(x1_dram[t - 1], xt[(t - 1) % 2]).then_inc(x1_out[(t - 1) % 2], 16)
            sp.wait_ge(x1_ready, NT)
            sp.dma_start(x1_dram[NT - 1], xt[(NT - 1) % 2]).then_inc(x1_out[(NT - 1) % 2], 16)
            sp.wait_ge(wq_in, 16)
            sp.wait_ge(x1_out[0], 16 * 5)
            sp.wait_ge(x1_out[1], 16 * 4)

        @block.tensor
        def _(pe):
            for u, (i, t) in enumerate(units):
                if t == 0:
                    pe.wait_ge(wg_in[i % 2], 48 * (i // 2 + 1))
                if u >= 3:
                    pe.wait_ge(prod, u - 2)
                c = slice(t * P, (t + 1) * P)
                for k in range(KC):
                    nc.tensor.matmul(ps[:, u % 3, :], hT[:, k, c], wg[:, i % 2, k, :], start=(k == 0), stop=(k == KC - 1))
                for k in range(4):
                    last = nc.tensor.matmul(ps[:, 3 + u % 3, :], oT[steps[i][1]][:, k, c], wo[:, i % 2, k, :], start=(k == 0), stop=(k == 3))
                last.then_inc(gate, 1)
            pe.wait_ge(mix, N)

            def turn(t):
                if t >= 2:
                    pe.wait_ge(mt_kept, t - 1)
                for c in range(KC):
                    last = nc.tensor.transpose(ps[:, 4 + 2 * (t % 2) + c // 4, (c % 4) * P:(c % 4 + 1) * P], mixed[:, t, c * P:(c + 1) * P], ident)
                last.then_inc(mt_T, 1)

            turn(0)
            for t in range(NT):
                if t + 1 < NT:
                    turn(t + 1)
                pe.wait_ge(mt_kept, t + 1)
                if t == 0:
                    for i in range(2):
                        pe.wait_ge(wg_in[i], 48 * 3 + 16)
                if t >= 2:
                    pe.wait_ge(x1_ready, t - 1)
                for n in range(2):
                    for k in range(KC):
                        last = nc.tensor.matmul(ps[:, 2 * (t % 2) + n, :], mT[t % 2][:, k, :], wg[:, n, k, :], start=(k == 0), stop=(k == KC - 1))
                last.then_inc(outp, 1)

        @block.scalar
        def _(act):
            for u in range(N):
                act.wait_ge(gbias, u + 1)
                nc.scalar.activation(gt[:, u % 3, :], gt[:, u % 3, :], ACT.Sigmoid).then_inc(sig, 1)
            for t in range(NT):
                act.wait_ge(mt_T, t + 1)
                if t >= 2:
                    act.wait_ge(outp, t - 1)
                b = 4 + 2 * (t % 2)
                nc.scalar.activation(mT[t % 2], ps[:, b:b + 2, :].rearrange("p a (c n) -> p (a c) n", n=P), ACT.Copy).then_inc(mt_kept, 1)

        @block.vector
        def _(dve):
            dve.wait_ge(bg_in, 16)

            def front(u):
                i, t = units[u]
                n, b = steps[i]
                dve.wait_ge(gate, u + 1)
                if u >= 3:
                    dve.wait_ge(mix, u - 2)
                o = b * DM + n * HB
                nc.vector.tensor_tensor(gt[:, u % 3, :], ps[:, u % 3, :], bg[:, o:o + HB], ALU.add).then_inc(gbias, 1)

            def back(u):
                i, t = units[u]
                n, b = steps[i]
                m = mixed[:, t, n * HB:(n + 1) * HB]
                dve.wait_ge(sig, u + 1)
                dst = m if b == 0 else gt[:, u % 3, :]
                nc.vector.tensor_tensor(dst, gt[:, u % 3, :], ps[:, 3 + u % 3, :], ALU.mult).then_inc(prod, 1)
                dve.wait_ge(prod, u + 1)
                if b == 0:
                    dve.sem_inc(mix, 1)
                else:
                    nc.vector.tensor_tensor(m, m, gt[:, u % 3, :], ALU.add).then_inc(mix, 1)

            for u in range(N):
                front(u)
                if u >= 1:
                    back(u - 1)
            back(N - 1)
            for t in range(NT):
                dve.wait_ge(outp, t + 1)
                dve.wait_ge(xt_in[t % 2], 16 * (t // 2 + 1))
                b = 2 * (t % 2)
                nc.vector.tensor_tensor(xt[t % 2], xt[t % 2], ps[:, b:b + 2, :].rearrange("p a n -> p (a n)"), ALU.add).then_inc(x1_ready, 1)


EARLY = SLOTS - RING
STEP_AT = {2: 0, 3: 1, 4: 2, 5: 3, 7: 4, 8: 11, 9: 5, 11: 6, 12: 12, 13: 7, 15: 8, 16: 13, 17: 9, 19: 10, 20: 14}
PROLOGUE = (3, 4, 11, 5, 6, 12, 7, 8, 13, 9, 10, 14)
TOP_FROM, TOP_BATCHES = 9, 20
FINISH_AT = 29
STEP_AT_FIRST = {2: 0, 3: 1, 4: 2, 5: 3, 7: 4, 9: 5, 10: 6, 11: 7, 12: 8, 13: 9, 14: 10, 15: 11, 16: 12, 17: 13, 18: 14}
TOP_FROM_FIRST, TOP_BATCHES_FIRST = 16, 13


def top_pieces(q, start, batches):
    c = q - start
    n = 3 * PH
    if not 0 <= c < batches:
        return []
    return [(i // 3, i % 3) for i in range(c * n // batches, (c + 1) * n // batches)]


def peer(nc, A, S, x1_dram):
    ident, ps = S["const"][:, 0:P], S["ps"]
    iota = S["const"][:, 5 * P:5 * P + TOPK]
    with ExitStack() as ctx:
        sb = lambda n, s, dt=F32: ctx.enter_context(nc.sbuf_tensor(n, s, dt))
        sem = lambda n: ctx.enter_context(nc.semaphore(n))
        wq = S["wq"]
        keysT, qT = (S["rest"][:, i * WQ:(i + 1) * WQ].rearrange("p (a n) -> p a n", n=P) for i in range(2))
        s = S["rest"][:, 2 * WQ:3 * WQ]
        ring = sb("ring", [P, RING, 2 * DM])
        gffn = sb("gffn", [P, DM])
        x1n = sb("x1n", [P, DM])
        x1c = sb("x1c", [P, DM])
        xn = sb("xn", [P, DM])
        xnT = sb("xnT", [P, KC, P])
        yout = sb("yout", [P, DM])
        rep = sb("rep", [P, TOPK * TOPK])
        rep2 = sb("rep2", [P, TOPK * TOPK])
        cand = sb("cand", [P, TOPK * TOPK])
        hot = sb("hot", [P, 2, TOPK, TOPK])
        v16 = sb("v16", [P, 2, TOPK])
        i16 = sb("i16", [P, 2, TOPK], U32)
        i16f = sb("i16f", [P, 2, TOPK])
        flat = sb("flat", [P, TOPK], U32)
        part = sb("part", [P, 2, TOPK], U32)
        partf = sb("partf", [P, 2, TOPK])
        e12 = sb("e12", [P, 2, TOPK])
        best = sb("best", [P, PH, TOPK])
        bsum = sb("bsum", [P, 2, PH])
        nrm = sb("p_nrm", [P, 4])
        idxn = sb("idxn", [P, SLOTS], U32)
        idx = sb("idx", [P, SLOTS], U32)
        gwn = sb("gwn", [P, SLOTS])
        gw = sb("gw", [P, SLOTS])
        hid = sb("hid", [P, SLOTS])
        act_ = sb("act_", [P, SLOTS])
        wgt = sb("wgt", [P, SLOTS])
        diag = sb("diag", [P, 2 * BATCH, P])

        keys_in = sem("keys_in")
        gffn_in = sem("gffn_in")
        keys_T = sem("keys_T")
        keys_kept = sem("keys_kept")
        ring_in = [sem(f"ring_in{r}") for r in range(RING)]
        slot_free = sem("slot_free")
        tail_taken = sem("tail_taken")
        copies = sem("copies")
        dots = sem("dots")
        gelus = sem("gelus")
        weights = sem("weights")
        diags = sem("diags")
        x1c_in = sem("x1c_in")
        y_out = sem("y_out")
        y_free = sem("y_free")
        x1n_in = sem("x1n_in")
        p_sq = sem("p_sq")
        p_ms = sem("p_ms")
        p_rt = sem("p_rt")
        acc_free = sem("acc_free")
        p_xn = sem("p_xn")
        p_xT = sem("p_xT")
        p_xkept = sem("p_xkept")
        p_q = sem("p_q")
        p_qkept = sem("p_qkept")
        p_s = sem("p_s")
        p_skept = sem("p_skept")
        p_shift = sem("p_shift")
        p_exp = sem("p_exp")
        link_ = sem("link_")
        prepared = sem("prepared")
        head_ready = sem("head_ready")
        h_shift = sem("h_shift")
        h_exp = sem("h_exp")
        s_free = sem("s_free")
        dve_turn = sem("dve_turn")
        pool_turn = sem("pool_turn")

        NB = SLOTS // BATCH
        acc = ps[:, 2:4, :]
        xp = ps[:, 0:2, :].rearrange("p a n -> p (a n)")
        y_v = A["y_prompt"][0].rearrange("(t p) n -> t p n", p=P)
        block = ctx.enter_context(nc.Block())

        @block.sync
        def _(sp):
            sp.dma_start(x1n[:, :], x1_dram[0]).then_inc(x1n_in, 16)
            sp.dma_start(gffn[:, :], A["norm_ffn"][0:1, :].to_broadcast([P, DM])).then_inc(gffn_in, 16)
            sp.dma_start(ring[:, 0, :].rearrange("p (a d) -> p a d", d=P), A["peer_keys"][0].rearrange("h a k d -> k (h a) d")).then_inc(keys_in, 16)
            sp.dma_start(x1c[:, :], x1_dram[0]).then_inc(x1c_in, 16)
            sp.sem_inc(y_free, 1)

            def tile(m, last):
                if not last:
                    sp.wait_ge(p_xn, m + 1)
                    sp.dma_start(x1n[:, :], x1_dram[m + 1]).then_inc(x1n_in, 16)
                sp.wait_ge(acc_free, m + 2)
                dst = A["y_sample"].rearrange("b s n -> (b s) n") if last else y_v[m]
                sp.dma_start(dst, yout[:, :]).then_inc(y_out, 16)
                sp.wait_ge(y_out, 16 * m + 16)
                sp.sem_inc(y_free, 1)
                if not last:
                    sp.dma_start(x1c[:, :], x1_dram[m + 1]).then_inc(x1c_in, 16)

            with sp.Fori(0, PT) as m:
                tile(m, False)
            tile(ST, True)

        @block.gpsimd
        def _(pool):
            def tile(m, first):
                if not first:
                    pool.wait_ge(prepared, m + 1)
                for j in range(SLOTS):
                    if first and j % TOPK == 0:
                        pool.wait_ge(head_ready, j // TOPK + 1)
                    if not first and j == EARLY:
                        pool.wait_ge(tail_taken, m + 1)
                    pool.wait_ge(slot_free, m * SLOTS + j + 1)
                    pool.sem_inc(pool_turn, 1)
                    i = nc.gpsimd.indirect_dma_start(out=ring[:, j % RING, :], out_offset=None, in_=A["experts"],
                                                     in_offset=bass.IndirectOffsetOnAxis(ap=idx[:, j:j + 1], axis=0))
                    i.then_inc(ring_in[j % RING], 16)

            tile(0, True)
            with pool.Fori(1, NT) as m:
                tile(m, False)

        @block.tensor
        def _(pe):
            pe.sem_inc(slot_free, RING)
            def prepare(n, g):
                if g == 2:
                    pe.wait_ge(p_xn, n + 1)
                    for c in range(KC):
                        last = nc.tensor.transpose(ps[:, 4 + c // 4, (c % 4) * P:(c % 4 + 1) * P], xn[:, c * P:(c + 1) * P], ident)
                    last.then_inc(p_xT, 1)
                if 3 <= g < 11:
                    b = (g - 3) // 2
                    pe.wait_ge(p_xkept, n + 1)
                    if b >= 2:
                        pe.wait_ge(p_qkept, n * 4 + b - 1)
                    for a in range(2 * (g - 3), 2 * (g - 3) + 2):
                        for k in range(KC):
                            last = nc.tensor.matmul(ps[:, 4 + b % 2, (a % 4) * P:(a % 4 + 1) * P], wq[:, k, a * P:(a + 1) * P], xnT[:, k, :],
                                                    start=(k == 0), stop=(k == KC - 1))
                    if g % 2 == 0:
                        last.then_inc(p_q, 1)
                if 11 <= g < 15:
                    b = g - 11
                    pe.wait_ge(p_qkept, n * 4 + b + 1)
                    if b >= 2:
                        pe.wait_ge(p_skept, n * 4 + b - 1)
                    for a in range(4):
                        last = nc.tensor.matmul(ps[:, 6 + b % 2, a * P:(a + 1) * P], qT[:, 4 * b + a, :], keysT[:, 4 * b + a, :], start=True, stop=True)
                    last.then_inc(p_s, 1)

            def tile(m, last_tile, step_at=STEP_AT):
                for q in range(NB):
                    pe.wait_ge(diags, m * NB + q + 1)
                    if q == 0:
                        pe.wait_ge(acc_free, m + 1)
                    for j in range(q * BATCH, (q + 1) * BATCH):
                        for h in range(2):
                            last = nc.tensor.matmul(acc[:, h, :], diag[:, j % (2 * BATCH), :], ring[:, j % RING, DM + h * HB:DM + (h + 1) * HB],
                                                    start=(j == 0), stop=(j == SLOTS - 1), skip_group_check=True)
                        last.then_inc(slot_free, 1)
                    if q == NB // 2:
                        pe.wait_ge(x1c_in, 16 * m + 16)
                        for h in range(2):
                            nc.tensor.matmul(acc[:, h, :], ident, x1c[:, h * HB:(h + 1) * HB], start=False, stop=False, skip_group_check=True)
                    if q in step_at and not last_tile:
                        prepare(m + 1, step_at[q])

            prepare(0, 2)
            pe.wait_ge(keys_in, 16)
            for a in range(2 * PH):
                last = nc.tensor.transpose(ps[:, a // 4, (a % 4) * P:(a % 4 + 1) * P], ring[:, 0, a * P:(a + 1) * P], ident)
            last.then_inc(keys_T, 1)
            pe.wait_ge(keys_kept, 1)
            for g in PROLOGUE:
                prepare(0, g)
            tile(0, False, STEP_AT_FIRST)
            with pe.Fori(1, PT) as m:
                tile(m, False)
            tile(ST, True)

        @block.scalar
        def _(act):
            def prepare(n, g):
                if g == 0:
                    act.wait_ge(x1n_in, 16 * n + 16)
                    nc.scalar.activation(qT[:, 0:KC, :].rearrange("p a n -> p (a n)"), x1n[:, :], ACT.Square, accum_out=nrm[:, 0:1]).then_inc(p_sq, 1)
                    act.wait_ge(p_ms, n + 1)
                    nc.scalar.activation(nrm[:, 2:3], nrm[:, 1:2], ACT.Sqrt).then_inc(p_rt, 1)
                if g == 2:
                    act.wait_ge(p_xT, n + 1)
                    nc.scalar.activation(xnT[:, :, :], ps[:, 4:6, :].rearrange("p a (c n) -> p (a c) n", n=P), ACT.Copy).then_inc(p_xkept, 1)
                if 3 <= g < 11 and g % 2 == 0:
                    b = (g - 3) // 2
                    act.wait_ge(p_q, n * 4 + b + 1)
                    nc.scalar.activation(qT[:, b * 4:(b + 1) * 4, :], ps[:, 4 + b % 2, :].rearrange("p (a n) -> p a n", n=P), ACT.Copy).then_inc(p_qkept, 1)
                if 11 <= g < 15:
                    b = g - 11
                    act.wait_ge(p_s, n * 4 + b + 1)
                    if b == 0:
                        act.wait_ge(s_free, n + 1)
                    nc.scalar.activation(s[:, b * HB:(b + 1) * HB], ps[:, 6 + b % 2, :], ACT.Copy).then_inc(p_skept, 1)
                if g == 15:
                    act.wait_ge(p_shift, n + 1)
                    nc.scalar.activation(best[:, :, :], best[:, :, :], ACT.Exp).then_inc(p_exp, 1)

            def exp_first(h):
                act.wait_ge(h_shift, h + 1)
                nc.scalar.activation(best[:, h, :], best[:, h, :], ACT.Exp).then_inc(h_exp, 1)

            def tile(m, last_tile, step_at=STEP_AT, first=False):
                for q in range(NB):
                    c = slice(q * BATCH, (q + 1) * BATCH)
                    act.wait_ge(dots, m * NB + q + 1)
                    nc.scalar.activation(act_[:, c], hid[:, c], ACT.Gelu_apprx_tanh).then_inc(gelus, 1)
                    act.wait_ge(weights, m * NB + q + 1)
                    if q >= 2:
                        act.wait_ge(slot_free, m * SLOTS + RING + (q - 1) * BATCH)
                    else:
                        act.wait_ge(slot_free, m * SLOTS + RING - (2 - q) * BATCH + BATCH)
                    for j in range(q * BATCH, (q + 1) * BATCH):
                        last = nc.scalar.activation(diag[:, j % (2 * BATCH), :], ident, ACT.Copy, scale=wgt[:, j:j + 1])
                    last.then_inc(diags, 1)
                    if q in step_at and not last_tile:
                        prepare(m + 1, step_at[q])
                    if first and q % 2 == 1 and q < 2 * PH - 2:
                        exp_first(q // 2 + 1)
                    if q == FINISH_AT and not last_tile:
                        prepare(m + 1, 15)
                act.wait_ge(slot_free, m * SLOTS + SLOTS + RING)
                act.wait_ge(y_free, m + 1)
                nc.scalar.activation(yout[:, :], acc.rearrange("p a n -> p (a n)"), ACT.Copy).then_inc(acc_free, 1)

            act.sem_inc(acc_free, 1)
            prepare(0, 0)
            prepare(0, 2)
            act.wait_ge(keys_T, 1)
            nc.scalar.activation(keysT[:, :, :].rearrange("p a n -> p (a n)"), ps[:, 0:4, :].rearrange("p a n -> p (a n)"), ACT.Copy).then_inc(keys_kept, 1)
            for g in PROLOGUE:
                prepare(0, g)
                if g == 12:
                    exp_first(0)
            act.sem_inc(p_exp, 1)
            tile(0, False, STEP_AT_FIRST, True)
            with act.Fori(1, PT) as m:
                tile(m, False)
            tile(ST, True)

        @block.vector
        def _(dve):
            dve.wait_ge(gffn_in, 16)
            dve.sem_inc(s_free, 1)
            linked = [0]

            def link(ins):
                linked[0] += 1
                ins.then_inc(link_, 1)
                dve.wait_ge(link_, linked[0])

            def prepare(n, step, pieces, finish, ids=idxn):
                if step == 0:
                    linked[0] = 0
                    dve.sem_clear(link_)
                    dve.wait_ge(p_sq, n + 1)
                    nc.vector.tensor_scalar(nrm[:, 1:2], nrm[:, 0:1], 1.0 / DM, EPS, ALU.mult, ALU.add).then_inc(p_ms, 1)
                if step == 1:
                    dve.wait_ge(p_rt, n + 1)
                    link(nc.vector.reciprocal(nrm[:, 3:4], nrm[:, 2:3]))
                    nc.vector.scalar_tensor_tensor(out=xn[:, :], in0=x1n[:, :], scalar=nrm[:, 3:4], in1=gffn[:, :],
                                                   op0=ALU.mult, op1=ALU.mult).then_inc(p_xn, 1)
                for h, piece in pieces:
                    if h % 2 == 0 and piece == 0:
                        dve.wait_ge(p_skept, n * 4 + h // 2 + 1)
                        dve.sem_inc(dve_turn, 1)
                    if piece < 2:
                        p = piece
                        sv = s[:, (2 * h + p) * NK:(2 * h + p + 1) * NK]
                        link(nc.vector.max(v16[:, p, 0:8], sv))
                        nc.vector.max_index(i16[:, p, 0:8], v16[:, p, 0:8], sv)
                        link(nc.vector.match_replace(rep[:, 0:NK], v16[:, p, 0:8], sv, -3.0e38))
                        link(nc.vector.max(v16[:, p, 8:16], rep[:, 0:NK]))
                        link(nc.vector.max_index(i16[:, p, 8:16], v16[:, p, 8:16], rep[:, 0:NK]))
                        continue
                    c3 = cand[:, :].rearrange("p (i j) -> p i j", i=TOPK)
                    link(nc.vector.tensor_tensor(c3, v16[:, 0, :].unsqueeze(2).to_broadcast([P, TOPK, TOPK]),
                                                 v16[:, 1, :].unsqueeze(1).to_broadcast([P, TOPK, TOPK]), ALU.add))
                    nc.vector.tensor_copy(i16f[:, :, :], i16[:, :, :])
                    link(nc.vector.max(best[:, h, 0:8], cand[:, :]))
                    nc.vector.max_index(flat[:, 0:8], best[:, h, 0:8], cand[:, :])
                    link(nc.vector.match_replace(rep2[:, :], best[:, h, 0:8], cand[:, :], -3.0e38))
                    link(nc.vector.max(best[:, h, 8:16], rep2[:, :]))
                    link(nc.vector.max_index(flat[:, 8:16], best[:, h, 8:16], rep2[:, :]))
                    link(nc.vector.tensor_scalar(part[:, 0, :], flat[:, :], 4, None, ALU.logical_shift_right))
                    link(nc.vector.tensor_scalar(part[:, 1, :], flat[:, :], 15, None, ALU.bitwise_and))
                    link(nc.vector.tensor_copy(partf[:, :, :], part[:, :, :]))
                    link(nc.vector.tensor_tensor(hot[:, :, :, :].rearrange("p a k i -> p (a k) i"),
                                                 partf[:, :, :].rearrange("p a k -> p (a k)").unsqueeze(2).to_broadcast([P, 2 * TOPK, TOPK]),
                                                 iota.unsqueeze(1).to_broadcast([P, 2 * TOPK, TOPK]), ALU.is_equal))
                    link(nc.vector.tensor_tensor(hot[:, :, :, :], hot[:, :, :, :],
                                                 i16f[:, :, :].unsqueeze(2).to_broadcast([P, 2, TOPK, TOPK]), ALU.mult))
                    link(nc.vector.tensor_reduce(e12[:, :, :].rearrange("p a k -> p (a k)"), hot[:, :, :, :].rearrange("p a k i -> p (a k) i"), AX, ALU.add))
                    link(nc.vector.scalar_tensor_tensor(out=ids[:, h * TOPK:(h + 1) * TOPK], in0=e12[:, 0, :], scalar=float(NK), in1=e12[:, 1, :],
                                                        op0=ALU.mult, op1=ALU.add))
                if finish:
                    link(nc.vector.tensor_copy(bsum[:, 1, :], best[:, :, 0]))
                    nc.vector.tensor_tensor(best[:, :, :], best[:, :, :], bsum[:, 1, :].unsqueeze(2).to_broadcast([P, PH, TOPK]), ALU.subtract).then_inc(p_shift, 1)
                    dve.wait_ge(p_exp, n + 1)
                    link(nc.vector.tensor_reduce(bsum[:, 0, :], best[:, :, :], AX, ALU.add))
                    link(nc.vector.reciprocal(bsum[:, 1, :], bsum[:, 0, :]))
                    link(nc.vector.tensor_tensor(gwn[:, :].rearrange("p (h k) -> p h k", h=PH), best[:, :, :],
                                                 bsum[:, 1, :].unsqueeze(2).to_broadcast([P, PH, TOPK]), ALU.mult))
                    link(nc.vector.tensor_copy(idx[:, 0:EARLY], idxn[:, 0:EARLY]))
                    dve.sem_inc(prepared, 1)
                    dve.sem_inc(s_free, 1)

            def finish_first(h):
                link(nc.vector.tensor_copy(bsum[:, 1, h:h + 1], best[:, h, 0:1]))
                nc.vector.tensor_tensor(best[:, h, :], best[:, h, :], bsum[:, 1, h:h + 1].to_broadcast([P, TOPK]), ALU.subtract).then_inc(h_shift, 1)
                dve.wait_ge(h_exp, h + 1)
                link(nc.vector.tensor_reduce(bsum[:, 0, h:h + 1], best[:, h, :], AX, ALU.add))
                link(nc.vector.reciprocal(bsum[:, 1, h:h + 1], bsum[:, 0, h:h + 1]))
                link(nc.vector.tensor_tensor(gw[:, h * TOPK:(h + 1) * TOPK], best[:, h, :], bsum[:, 1, h:h + 1].to_broadcast([P, TOPK]), ALU.mult))
                dve.sem_inc(head_ready, 1)
                if h == PH - 1:
                    dve.sem_inc(s_free, 1)

            def tile(m, last_tile, first=False):
                if first:
                    dve.sem_inc(copies, 1)
                else:
                    nc.vector.tensor_copy(idx[:, EARLY:SLOTS], idxn[:, EARLY:SLOTS]).then_inc(tail_taken, 1)
                    nc.vector.tensor_copy(gw[:, :], gwn[:, :]).then_inc(copies, 1)
                nc.vector.tensor_copy(xp, xn[:, :]).then_inc(copies, 1)
                dve.wait_ge(copies, m * 2 + 2)
                if not first:
                    dve.wait_ge(tail_taken, m + 1)
                for q in range(NB):
                    for j in range(q * BATCH, (q + 1) * BATCH):
                        dve.wait_ge(ring_in[j % RING], m * (16 * SLOTS // RING) + 16 * (j // RING + 1))
                        u = ring[:, j % RING, 0:DM]
                        last = nc.vector.tensor_tensor_reduce(out=u, in0=u, in1=xp, scale=1.0, scalar=0.0, op0=ALU.mult, op1=ALU.add,
                                                              accum_out=hid[:, j:j + 1])
                    last.then_inc(dots, 1)
                    dve.wait_ge(gelus, m * NB + q + 1)
                    c = slice(q * BATCH, (q + 1) * BATCH)
                    nc.vector.tensor_tensor(wgt[:, c], act_[:, c], gw[:, c], ALU.mult).then_inc(weights, 1)
                    if first and q < 2 * PH - 2:
                        h = q // 2 + 1
                        prepare(0, None, [(h, 0), (h, 1)] if q % 2 == 0 else [(h, 2)], False, idx)
                        if q % 2 == 1:
                            finish_first(h)
                    if first:
                        prepare(1, STEP_AT_FIRST.get(q), top_pieces(q, TOP_FROM_FIRST, TOP_BATCHES_FIRST), q == FINISH_AT)
                    elif not last_tile:
                        prepare(m + 1, STEP_AT.get(q), top_pieces(q, TOP_FROM, TOP_BATCHES), q == FINISH_AT)
                dve.wait_ge(weights, m * NB + NB)

            prepare(0, 0, [], False)
            prepare(0, 1, [(0, 0), (0, 1), (0, 2)], False, idx)
            finish_first(0)
            dve.sem_inc(prepared, 1)
            dve.sem_inc(tail_taken, 1)
            dve.sem_inc(p_shift, 1)
            tile(0, False, True)
            with dve.Fori(1, PT) as m:
                tile(m, False)
            tile(ST, True)


def build(nc, A, small_dram, wide_dram):
    with ExitStack() as top:
        S = {}
        S["const"] = top.enter_context(nc.sbuf_tensor("const", [P, CW], F32))
        S["ps"] = top.enter_context(nc.psum_tensor("ps", [P, 8, HB], F32))
        x1_dram = nc.dram_tensor("x1_scratch", (NT, P, DM), F32, kind="Internal").ap()

        def hold(stack, name, shape):
            S[name] = stack.enter_context(nc.sbuf_tensor(name, shape, F32))

        room = top.enter_context(nc.sbuf_tensor("room", [P, 20 * TOK], F32))
        S["wq"] = room[:, 0:KC * WQ].rearrange("p (c n) -> p c n", c=KC)
        S["rest"] = room[:, KC * WQ:20 * TOK]
        if True:
            for i, n in enumerate(("qsbT", "qswT", "qmT")):
                S[n] = room[:, i * 4 * TOK:(i + 1) * 4 * TOK].rearrange("p (j t) -> p j t", j=4)
            S["hT"] = room[:, 12 * TOK:20 * TOK].rearrange("p (c t) -> p c t", c=KC)
            with ExitStack() as kv:
                hold(kv, "kswT", [P, (NT + 1) * P])
                hold(kv, "vsw", [P, NT + 1, P])
                hold(kv, "mkT", [P, MH, MT])
                hold(kv, "mv", [P, 2, MH * MD])
                with ExitStack() as sbkv:
                    hold(sbkv, "ksbT", [P, 4, TOK])
                    hold(sbkv, "vsb", [P, NT, SB_W])
                    with ExitStack() as first:
                        hold(first, "mhT", [P, KC, MT])
                        project(nc, A, S, small_dram)
                    stick(nc, A, S)
                windows(nc, A, S, wide_dram)
            merge(nc, A, S, x1_dram)
        peer(nc, A, S, x1_dram)


_INS = ["x_prompt", "mem_prompt", "x_sample", "cache_sb_k", "cache_sb_v", "cache_swa_k", "cache_swa_v",
        "cache_mem_k", "cache_mem_v", "norm_mix", "w_in", "b_gate", "q_norm_sw", "k_norm_sw", "sinks", "norm_mem",
        "w_mem_kv", "q_norm_mem", "k_norm_mem", "w_o_sb", "w_o_sw", "w_o_mem", "w_out", "norm_ffn", "w_peer_q",
        "peer_keys"]
_OUTS = {"y_prompt": (1, 1024, 1024), "y_sample": (8, 16, 1024),
         "new_sb_k_prompt": (1, 1, 1024, 8, 64), "new_sb_v_prompt": (1, 1, 1024, 8, 64),
         "new_swa_k_prompt": (1, 1, 128, 2, 64), "new_swa_v_prompt": (1, 1, 128, 2, 64),
         "new_mem_k_prompt": (1, 1, 256, 4, 128), "new_mem_v_prompt": (1, 1, 256, 4, 128),
         "new_sb_k_sample": (1, 8, 16, 8, 64), "new_sb_v_sample": (1, 8, 16, 8, 64),
         "new_swa_k_sample": (1, 8, 128, 2, 64), "new_swa_v_sample": (1, 8, 128, 2, 64)}


def kernel(**inputs):
    import numpy as _np
    import concourse.bacc as _bacc
    from concourse import mybir as _mybir
    from concourse.bass_utils import run_bass_kernel_spmd as _run

    nc = _bacc.Bacc("TRN2", target_bir_lowering=False, num_devices=1)
    arrays, A = {}, {}

    def give(name, a):
        a = _np.ascontiguousarray(a)
        arrays[f"in_{name}_dram"] = a
        return nc.dram_tensor(f"in_{name}_dram", a.shape, _mybir.dt.from_np(a.dtype), kind="ExternalInput").ap()

    for name in _INS:
        A[name] = give(name, inputs[name])
    A["experts"] = give("experts", _np.concatenate([_np.asarray(inputs["peer_u"][0]), _np.asarray(inputs["peer_v"][0])], axis=1))
    small, wide = host_constants()
    small_dram, wide_dram = give("small", small), give("wide", wide)
    for name, shape in _OUTS.items():
        A[name] = nc.dram_tensor(f"out_{name}", shape, _mybir.dt.from_np(_np.dtype("float32")), kind="ExternalOutput").ap()
    build(nc, A, small_dram, wide_dram)
    r = _run(nc, [arrays], core_ids=[0])
    return tuple(r.results[0][f"out_{name}"] for name in _OUTS)
```
